# Optimizing a Trainium2 kernel written in Bass

```python
import math
import jax, jax.numpy as jnp
from jax import lax
import numpy as np
import jax
import jax.numpy as jnp

D_MODEL = 1024
BATCH = 1
SEQ = 256
DEPTH = 2

N_MIXERS = 2
CONV_WIDTH = 3
HEAD_DIM = 64
N_Q_HEADS = D_MODEL // HEAD_DIM
N_KV_HEADS = 4
GROUP = N_Q_HEADS // N_KV_HEADS
WINDOW = 128
BLOCK = 128
D_FF = ((8 * D_MODEL // 3 + 255) // 256) * 256
QKV_WIDTH = (N_Q_HEADS + 2 * N_KV_HEADS) * HEAD_DIM
N_CONV_LAYERS = (DEPTH + 1) // 2
N_ATTN_LAYERS = DEPTH // 2
EPS = 1e-6


def rmsnorm(x, gain):
    xf = x.astype(jnp.float32)
    r = lax.rsqrt(jnp.mean(xf * xf, axis=-1, keepdims=True) + EPS)
    return (xf * r).astype(x.dtype) * gain

def alibi_slopes():
    h = jnp.arange(1, N_Q_HEADS + 1, dtype=jnp.float32)
    return jnp.exp2(-8.0 * h / N_Q_HEADS)

def short_conv_mixer(h, w_in, conv_w, w_out):
    d = h.shape[-1]
    bcx = h @ w_in
    b_gate, c_gate, xv = jnp.split(bcx, 3, axis=-1)
    u = b_gate * xv
    y = lax.conv_general_dilated(
        u, conv_w[:, None, :].astype(u.dtype),
        window_strides=(1,), padding=[(CONV_WIDTH - 1, 0)],
        dimension_numbers=('NWC', 'WIO', 'NWC'), feature_group_count=d)
    return (c_gate * y) @ w_out

def swa_sink_attention(h, w_qkv, q_gain, k_gain, sinks, w_o):
    bsz, s, _ = h.shape
    nb = s // BLOCK
    qkv = h @ w_qkv
    q_end = N_Q_HEADS * HEAD_DIM
    k_end = q_end + N_KV_HEADS * HEAD_DIM
    q = qkv[..., :q_end].reshape(bsz, s, N_KV_HEADS, GROUP, HEAD_DIM)
    k = qkv[..., q_end:k_end].reshape(bsz, s, N_KV_HEADS, HEAD_DIM)
    v = qkv[..., k_end:].reshape(bsz, s, N_KV_HEADS, HEAD_DIM)
    q = rmsnorm(q, q_gain)
    k = rmsnorm(k, k_gain)

    qb = q.reshape(bsz, nb, BLOCK, N_KV_HEADS, GROUP, HEAD_DIM)

    def band(t):
        tp = jnp.pad(t, ((0, 0), (BLOCK, 0), (0, 0), (0, 0)))
        tb = tp.reshape(bsz, nb + 1, BLOCK, N_KV_HEADS, HEAD_DIM)
        return jnp.concatenate([tb[:, :-1], tb[:, 1:]], axis=2)

    kw = band(k)
    vw = band(v)

    scale = 1.0 / math.sqrt(HEAD_DIM)
    scores = jnp.einsum('bnqkgd,bnskd->bnkgqs', qb, kw).astype(jnp.float32) * scale

    qi = jnp.arange(BLOCK)[:, None]
    kj = jnp.arange(2 * BLOCK)[None, :]
    dist = qi + BLOCK - kj
    key_pos = (jnp.arange(nb) * BLOCK - BLOCK)[:, None, None] + kj[None]
    mask = (dist >= 0)[None] & (dist < WINDOW)[None] & (key_pos >= 0)

    slopes = alibi_slopes().reshape(N_KV_HEADS, GROUP)
    alibi = -slopes[:, :, None, None] * dist.astype(jnp.float32)[None, None]
    scores = scores + alibi[None, None]
    scores = jnp.where(mask[None, :, None, None], scores, -jnp.inf)

    sink = sinks.astype(jnp.float32).reshape(N_KV_HEADS, GROUP)
    sink_col = jnp.broadcast_to(sink[None, None, :, :, None, None],
                                scores.shape[:-1] + (1,))
    logits = jnp.concatenate([scores, sink_col], axis=-1)
    p = jax.nn.softmax(logits, axis=-1)[..., :-1]

    out = jnp.einsum('bnkgqs,bnskd->bnqkgd', p.astype(vw.dtype), vw)
    out = out.reshape(bsz, s, N_Q_HEADS * HEAD_DIM)
    return out @ w_o

def swiglu_ffn(h, w_gate_up, w_down):
    gu = h @ w_gate_up
    g, u = jnp.split(gu, 2, axis=-1)
    return (jax.nn.silu(g) * u) @ w_down

def first_inputs(seed: int = 0) -> dict:
    key = jax.random.key(seed)
    ks = jax.random.split(key, 14)
    f32 = jnp.float32
    d = D_MODEL

    def w(k, shape, fan_in):
        return jax.random.normal(k, shape, f32) * (fan_in ** -0.5)

    return {
        "x": jax.random.normal(ks[0], (BATCH, SEQ, d), f32),
        "conv_w_in": w(ks[1], (N_CONV_LAYERS, d, 3 * d), d),
        "conv_w": w(ks[2], (N_CONV_LAYERS, CONV_WIDTH, d), CONV_WIDTH),
        "conv_w_out": w(ks[3], (N_CONV_LAYERS, d, d), d),
        "attn_w_qkv": w(ks[4], (N_ATTN_LAYERS, d, QKV_WIDTH), d),
        "attn_q_gain": 1.0 + 0.05 * jax.random.normal(ks[5], (N_ATTN_LAYERS, HEAD_DIM), f32),
        "attn_k_gain": 1.0 + 0.05 * jax.random.normal(ks[6], (N_ATTN_LAYERS, HEAD_DIM), f32),
        "attn_sinks": 0.5 * jax.random.normal(ks[7], (N_ATTN_LAYERS, N_Q_HEADS), f32),
        "attn_w_o": w(ks[8], (N_ATTN_LAYERS, N_Q_HEADS * HEAD_DIM, d), N_Q_HEADS * HEAD_DIM),
        "norm_mixer": 1.0 + 0.05 * jax.random.normal(ks[9], (DEPTH, d), f32),
        "norm_ffn": 1.0 + 0.05 * jax.random.normal(ks[10], (DEPTH, d), f32),
        "ffn_w_gate_up": w(ks[11], (DEPTH, d, 2 * D_FF), d),
        "ffn_w_down": w(ks[12], (DEPTH, D_FF, d), D_FF),
    }

def first_block(x, conv_w_in, conv_w, conv_w_out, attn_w_qkv, attn_q_gain, attn_k_gain,
              attn_sinks, attn_w_o, norm_mixer, norm_ffn, ffn_w_gate_up, ffn_w_down):
    for i in range(DEPTH):
        h = rmsnorm(x, norm_mixer[i])
        j = i // N_MIXERS
        if i % N_MIXERS == 0:
            mix = short_conv_mixer(h, conv_w_in[j], conv_w[j], conv_w_out[j])
        else:
            mix = swa_sink_attention(h, attn_w_qkv[j], attn_q_gain[j], attn_k_gain[j],
                                     attn_sinks[j], attn_w_o[j])
        x = x + mix
        h = rmsnorm(x, norm_ffn[i])
        x = x + swiglu_ffn(h, ffn_w_gate_up[i], ffn_w_down[i])
    return x


DEPTH_2 = 1

N_HEADS = 8
HEAD_DIM_2 = D_MODEL // N_HEADS
ATTN_WIDTH = N_HEADS * HEAD_DIM_2
ROT_DIM = HEAD_DIM_2 // 4
ROPE_THETA = 500000.0
MOBA_BLOCK = 256
MOBA_TOPK = 3
Q_CHUNK = 32
LRU_WIDTH = D_MODEL
LRU_BLOCKS = 4
LRU_BLOCK_WIDTH = LRU_WIDTH // LRU_BLOCKS
CONV_WIDTH_2 = 4
LRU_C = 8.0
D_FF_2 = 4 * D_MODEL
NORM_EPS = 1e-6
MASK_VALUE = -1e30
SPLITS = (ATTN_WIDTH, 2 * ATTN_WIDTH, 3 * ATTN_WIDTH,
          3 * ATTN_WIDTH + LRU_WIDTH, 3 * ATTN_WIDTH + 2 * LRU_WIDTH,
          3 * ATTN_WIDTH + 2 * LRU_WIDTH + D_MODEL)
IN_COLS = 3 * ATTN_WIDTH + 2 * LRU_WIDTH + 2 * D_MODEL


def rms_norm(x, gain):
    xf = x.astype(jnp.float32)
    y = xf * lax.rsqrt(jnp.mean(xf * xf, axis=-1, keepdims=True) + NORM_EPS)
    return (y * gain.astype(jnp.float32)).astype(x.dtype)

def rope_tables(seq_len):
    inv_freq = ROPE_THETA ** (-jnp.arange(0, ROT_DIM, 2, dtype=jnp.float32) / ROT_DIM)
    ang = jnp.arange(seq_len, dtype=jnp.float32)[:, None] * inv_freq[None, :]
    return jnp.cos(ang), jnp.sin(ang)

def partial_rope(x, cos, sin):
    half = ROT_DIM // 2
    x1 = x[..., :half].astype(jnp.float32)
    x2 = x[..., half:ROT_DIM].astype(jnp.float32)
    rot = jnp.concatenate([x1 * cos - x2 * sin, x2 * cos + x1 * sin], axis=-1).astype(x.dtype)
    return jnp.concatenate([rot, x[..., ROT_DIM:]], axis=-1)

def moba_attention(q, k, v):
    b, h, s, dh = q.shape
    n_blocks = -(-s // MOBA_BLOCK)
    pad = n_blocks * MOBA_BLOCK - s
    kp = jnp.pad(k, ((0, 0), (0, 0), (0, pad), (0, 0)))
    vp = jnp.pad(v, ((0, 0), (0, 0), (0, pad), (0, 0)))
    kb = kp.reshape(b, h, n_blocks, MOBA_BLOCK, dh)
    vb = vp.reshape(b, h, n_blocks, MOBA_BLOCK, dh)
    k_mean = jnp.mean(kb.astype(jnp.float32), axis=3)
    top = min(MOBA_TOPK, n_blocks)
    scale = dh ** -0.5
    n_chunks = s // Q_CHUNK
    q_chunks = jnp.moveaxis(q.reshape(b, h, n_chunks, Q_CHUNK, dh), 2, 0)
    block_ids = jnp.arange(n_blocks)
    gather_blocks = jax.vmap(jax.vmap(lambda blocks, idx: blocks[idx]))

    def one_chunk(args):
        c, qc = args
        q_start = c * Q_CHUNK
        q_pos = q_start + jnp.arange(Q_CHUNK)
        q_block = q_start // MOBA_BLOCK
        gate = jnp.einsum("bhqd,bhnd->bhqn", qc.astype(jnp.float32), k_mean)
        gate = jnp.where(block_ids < q_block, gate, -jnp.inf)
        _, sel = lax.top_k(gate, top)
        sel_ok = jnp.arange(top) < q_block
        k_sel = gather_blocks(kb, sel)
        v_sel = gather_blocks(vb, sel)
        s_sel = jnp.einsum("bhqd,bhqjkd->bhqjk", qc, k_sel).astype(jnp.float32) * scale
        s_sel = jnp.where(sel_ok[:, None], s_sel, MASK_VALUE)
        s_sel = s_sel.reshape(b, h, Q_CHUNK, top * MOBA_BLOCK)
        k_own = lax.dynamic_slice_in_dim(kp, q_block * MOBA_BLOCK, MOBA_BLOCK, axis=2)
        v_own = lax.dynamic_slice_in_dim(vp, q_block * MOBA_BLOCK, MOBA_BLOCK, axis=2)
        key_pos = q_block * MOBA_BLOCK + jnp.arange(MOBA_BLOCK)
        s_own = jnp.einsum("bhqd,bhkd->bhqk", qc, k_own).astype(jnp.float32) * scale
        s_own = jnp.where(key_pos[None, :] <= q_pos[:, None], s_own, MASK_VALUE)
        p = jax.nn.softmax(jnp.concatenate([s_sel, s_own], axis=-1), axis=-1).astype(v.dtype)
        p_sel = p[..., :top * MOBA_BLOCK].reshape(b, h, Q_CHUNK, top, MOBA_BLOCK)
        p_own = p[..., top * MOBA_BLOCK:]
        return (jnp.einsum("bhqjk,bhqjkd->bhqd", p_sel, v_sel)
                + jnp.einsum("bhqk,bhkd->bhqd", p_own, v_own))

    out = lax.map(one_chunk, (jnp.arange(n_chunks, dtype=jnp.int32), q_chunks))
    return jnp.moveaxis(out, 0, 2).reshape(b, h, s, dh)

def causal_depthwise_conv(x, w, bias):
    s = x.shape[1]
    xp = jnp.pad(x, ((0, 0), (CONV_WIDTH_2 - 1, 0), (0, 0)))
    y = bias
    for j in range(CONV_WIDTH_2):
        y = y + w[j] * xp[:, j:j + s]
    return y

def block_diag_linear(x, w, bias):
    b, s, _ = x.shape
    xg = x.reshape(b, s, LRU_BLOCKS, LRU_BLOCK_WIDTH)
    return jnp.einsum("bsgi,gij->bsgj", xg, w).reshape(b, s, LRU_WIDTH) + bias

def _linear_combine(left, right):
    a_l, b_l = left
    a_r, b_r = right
    return a_l * a_r, a_r * b_l + b_r

def rg_lru(x, w_a, b_a, w_i, b_i, lam):
    r = jax.nn.sigmoid(block_diag_linear(x, w_a, b_a).astype(jnp.float32))
    i = jax.nn.sigmoid(block_diag_linear(x, w_i, b_i).astype(jnp.float32))
    log_a = -LRU_C * r * jax.nn.softplus(-lam.astype(jnp.float32))
    a = jnp.exp(log_a)
    mult = jnp.sqrt(-jnp.expm1(2.0 * log_a))
    bx = mult * (i * x.astype(jnp.float32))
    _, h = lax.associative_scan(_linear_combine, (a, bx), axis=1)
    return h.astype(x.dtype)

def hybrid_mixer(u, w_in, conv_w, conv_b, w_rg_a, b_rg_a, w_rg_i, b_rg_i, lru_lambda,
                 w_branch_attn, w_branch_lru, w_out):
    b, s, _ = u.shape
    proj = jnp.einsum("bsd,dc->bsc", u, w_in)
    q, k, v, x_lru, g_lru, gate_attn, gate_lru = jnp.split(proj, list(SPLITS), axis=-1)

    def to_heads(t):
        return t.reshape(b, s, N_HEADS, HEAD_DIM_2).transpose(0, 2, 1, 3)

    cos, sin = rope_tables(s)
    qh = partial_rope(to_heads(q), cos, sin)
    kh = partial_rope(to_heads(k), cos, sin)
    attn = moba_attention(qh, kh, to_heads(v))
    attn = attn.transpose(0, 2, 1, 3).reshape(b, s, ATTN_WIDTH)
    y_attn = attn @ w_branch_attn

    xc = causal_depthwise_conv(x_lru, conv_w, conv_b)
    hl = rg_lru(xc, w_rg_a, b_rg_a, w_rg_i, b_rg_i, lru_lambda)
    y_lru = (hl * jax.nn.gelu(g_lru)) @ w_branch_lru

    merged = jax.nn.sigmoid(gate_attn) * y_attn + jax.nn.sigmoid(gate_lru) * y_lru
    return merged @ w_out

def second_inputs(seed: int = 0) -> dict:
    key = jax.random.key(seed)
    ks = jax.random.split(key, 18)
    f32 = jnp.float32

    def nrm(k, shape, scale):
        return jax.random.normal(k, shape, f32) * scale

    def gain(k):
        return 1.0 + 0.05 * jax.random.normal(k, (DEPTH_2, D_MODEL), f32)

    a_init = jax.random.uniform(ks[10], (DEPTH_2, LRU_WIDTH), f32, 0.9, 0.999)
    return {
        "x": nrm(ks[0], (BATCH, SEQ, D_MODEL), 1.0),
        "attn_pre_norm": gain(ks[1]),
        "attn_post_norm": gain(ks[2]),
        "w_in": nrm(ks[3], (DEPTH_2, D_MODEL, IN_COLS), D_MODEL ** -0.5),
        "conv_w": nrm(ks[4], (DEPTH_2, CONV_WIDTH_2, LRU_WIDTH), CONV_WIDTH_2 ** -0.5),
        "conv_b": nrm(ks[5], (DEPTH_2, LRU_WIDTH), 0.01),
        "w_rg_a": nrm(ks[6], (DEPTH_2, LRU_BLOCKS, LRU_BLOCK_WIDTH, LRU_BLOCK_WIDTH), LRU_BLOCK_WIDTH ** -0.5),
        "b_rg_a": nrm(ks[7], (DEPTH_2, LRU_WIDTH), 0.01),
        "w_rg_i": nrm(ks[8], (DEPTH_2, LRU_BLOCKS, LRU_BLOCK_WIDTH, LRU_BLOCK_WIDTH), LRU_BLOCK_WIDTH ** -0.5),
        "b_rg_i": nrm(ks[9], (DEPTH_2, LRU_WIDTH), 0.01),
        "lru_lambda": jnp.log(a_init) - jnp.log1p(-a_init),
        "w_branch_attn": nrm(ks[11], (DEPTH_2, ATTN_WIDTH, D_MODEL), ATTN_WIDTH ** -0.5),
        "w_branch_lru": nrm(ks[12], (DEPTH_2, LRU_WIDTH, D_MODEL), LRU_WIDTH ** -0.5),
        "w_out": nrm(ks[13], (DEPTH_2, D_MODEL, D_MODEL), D_MODEL ** -0.5),
        "mlp_pre_norm": gain(ks[14]),
        "mlp_post_norm": gain(ks[15]),
        "w_mlp_up": nrm(ks[16], (DEPTH_2, D_MODEL, D_FF_2), D_MODEL ** -0.5),
        "w_mlp_down": nrm(ks[17], (DEPTH_2, D_FF_2, D_MODEL), D_FF_2 ** -0.5),
    }

def second_block(x, attn_pre_norm, attn_post_norm, w_in, conv_w, conv_b, w_rg_a, b_rg_a,
              w_rg_i, b_rg_i, lru_lambda, w_branch_attn, w_branch_lru, w_out,
              mlp_pre_norm, mlp_post_norm, w_mlp_up, w_mlp_down):
    h = x
    for l in range(DEPTH_2):
        u = rms_norm(h, attn_pre_norm[l])
        mix = hybrid_mixer(u, w_in[l], conv_w[l], conv_b[l], w_rg_a[l], b_rg_a[l],
                           w_rg_i[l], b_rg_i[l], lru_lambda[l],
                           w_branch_attn[l], w_branch_lru[l], w_out[l])
        h = h + rms_norm(mix, attn_post_norm[l])
        u = rms_norm(h, mlp_pre_norm[l])
        m = jnp.square(jax.nn.relu(u @ w_mlp_up[l])) @ w_mlp_down[l]
        h = h + rms_norm(m, mlp_post_norm[l])
    return h


def setup_inputs(seed=0):
    out = dict(first_inputs(seed))
    for name, value in second_inputs(seed + 1).items():
        if name != "x":
            out[name + "_2"] = value
    return out


def reference(
    x, conv_w_in, conv_w, conv_w_out, attn_w_qkv, attn_q_gain, attn_k_gain, attn_sinks,
    attn_w_o, norm_mixer, norm_ffn, ffn_w_gate_up, ffn_w_down, attn_pre_norm_2,
    attn_post_norm_2, w_in_2, conv_w_2, conv_b_2, w_rg_a_2, b_rg_a_2, w_rg_i_2, b_rg_i_2,
    lru_lambda_2, w_branch_attn_2, w_branch_lru_2, w_out_2, mlp_pre_norm_2, mlp_post_norm_2,
    w_mlp_up_2, w_mlp_down_2,
):
    x = first_block(
        x, conv_w_in, conv_w, conv_w_out, attn_w_qkv, attn_q_gain, attn_k_gain, attn_sinks,
        attn_w_o, norm_mixer, norm_ffn, ffn_w_gate_up, ffn_w_down,
    )
    return second_block(
        x, attn_pre_norm_2, attn_post_norm_2, w_in_2, conv_w_2, conv_b_2, w_rg_a_2, b_rg_a_2,
        w_rg_i_2, b_rg_i_2, lru_lambda_2, w_branch_attn_2, w_branch_lru_2, w_out_2,
        mlp_pre_norm_2, mlp_post_norm_2, w_mlp_up_2, w_mlp_down_2,
    )


_drawn_inputs = setup_inputs


def setup_inputs(seed=0):
    import zlib

    import numpy as np

    out = dict(_drawn_inputs(seed))
    spreads = {}
    factors = {'attn_q_gain': 5.0,
     'attn_k_gain': 4.958,
     'attn_sinks': 27.234,
     'conv_b_2': 3.382,
     'b_rg_a_2': 58.897,
     'b_rg_i_2': 33.669,
     'mlp_post_norm_2': 2.728}
    for name, (base, spread) in spreads.items():
        noise = np.random.default_rng([zlib.crc32(name.encode()), seed]).standard_normal(out[name].shape)
        drawn = base * np.exp(spread * noise) if base else spread * noise
        out[name] = jnp.asarray(drawn.astype(out[name].dtype))
    for name, factor in factors.items():
        out[name] = (out[name] * factor).astype(out[name].dtype)
    return out
```

```python
from contextlib import ExitStack

import concourse.bass as bass
from concourse import mybir
import numpy as np

F32 = mybir.dt.float32
F32R = mybir.dt.float32r
ACT = mybir.ActivationFunctionType
ALU = mybir.AluOpType
AX = mybir.AxisListType

P = 128
TOK = 256
D = 1024
KT = D // P
EPS = 1e-6
FF = 2816
FT = FF // P
HEADS1, KV1, HD1 = 16, 4, 64
HEADS2, HD2 = 8, 128
FF2 = 4096
ROT = 32
PIECE = 8 * P
BIG = 1e30

BODIES = [("bx", 4), ("c", 2), ("o", 2), ("up0", 11), ("dn0", 6),
          ("qkv", 3), ("wo", 2), ("up1", 11), ("dn1", 6),
          ("x2", 2), ("q2", 2), ("k2", 2), ("rg", 1), ("v2", 2), ("g2", 2), ("ga", 2), ("gl", 2),
          ("ba", 2), ("bl", 2), ("out2", 2), ("mup", 8), ("mdn", 8)]
TILES = {"bx": 16, "c": 8, "o": 8, "up0": 44, "dn0": 8, "qkv": 12, "wo": 8, "up1": 44, "dn1": 8,
         "x2": 8, "q2": 8, "k2": 8, "rg": 16, "v2": 8, "g2": 8, "ga": 8, "gl": 8,
         "ba": 8, "bl": 8, "out2": 8, "mup": 32, "mdn": 8}
B0, T0 = {}, {}
_b = _t = 0
for _name, _n in BODIES:
    B0[_name], T0[_name] = _b, _t
    _b += _n
    _t += TILES[_name]
ALL_BODIES = _b
GROUP_K = [(0, 8), (8, 8), (16, 6)]


def blocks_of(n):
    for name in ("dn0", "dn1"):
        first = 4 * B0[name]
        if first <= n < first + 24:
            return GROUP_K[(n - first) // 2 % 3][1]
    return 8


def chunk_offset(c):
    short = 0
    for name in ("dn0", "dn1"):
        first = 2 * B0[name]
        short += sum(1 for j in range(4) if first + 3 * j + 2 < c)
    return c * 2 * P * PIECE - short * 2 * P * 2 * P


def vec_columns():
    at, out = 0, {}
    for name, n in [("mix0", 8), ("ffn0", 8), ("mix1", 8), ("ffn1", 8), ("conv", 24), ("qg", 1), ("kg", 1),
                    ("pre2", 8), ("post2", 8), ("conv2", 32), ("convb2", 8), ("ba", 8), ("bi", 8),
                    ("lam", 8), ("mpre", 8), ("mpost", 8)]:
        out[name] = at
        at += n
    return out, at


VEC, NVEC = vec_columns()
CON = {"ones": 0, "half": 128, "ident": 256, "mask": 384, "cos": 768, "sin": 1024, "rot": 1280}
NCON = 1280 + 32
PAIRS1 = HEADS1 // 2


def head1(i):
    tile, half = divmod(i, 2)
    return 4 * (2 * (tile // 4) + half) + tile % 4


def build(nc, bias_in_dram, x_in, stream, vecs_in, sinks_in, cons_in, out):
    with ExitStack() as ctx:
        sb = lambda n, s, d=F32: ctx.enter_context(nc.sbuf_tensor(n, s, d))
        sem = lambda n: ctx.enter_context(nc.semaphore(n))

        raw = sb("raw", [P, 4, 2 * PIECE])
        whi = sb("whi", [P, 4, 8, P], F32R)
        wlo = sb("wlo", [P, 4, 8, P], F32R)
        x = sb("x", [P, KT, TOK])
        xa = sb("xa", [P, KT, 2, TOK], F32R)
        xb = sb("xb", [P, KT, 2, TOK], F32R)
        spill = sb("spill", [P, 4, TOK])
        z = sb("z", [P, 4, TOK])
        act1 = sb("act1", [P, 2, TOK])
        gate = sb("gate", [P, 2, TOK])
        sq = sb("sq", [P, 2, TOK])
        ssum = sb("ssum", [P, TOK])
        rstd = sb("rstd", [P, TOK])
        rbc = sb("rbc", [P, TOK])
        vecs = sb("vecs", [P, NVEC])
        cons = sb("cons", [P, NCON])
        sinks = sb("sinks", [P, 4 * PAIRS1])
        nsinks = sb("nsinks", [P, 4 * PAIRS1])
        kgain = sb("kgain", [P, 1])
        lamb = sb("lamb", [P, 6, KT])
        lam8 = sb("lam8", [P, KT])
        nlam8 = sb("nlam8", [P, KT])
        rtmp = sb("rtmp", [ROT, 2, 2, TOK])
        rbc2 = sb("rbc2", [P, TOK])
        mx = sb("mx", [P, 2, 4])
        nmx = sb("nmx", [P, 2, 4])
        den = sb("den", [P, 2, 4])
        esink = sb("esink", [P, 2, 4])
        rden = sb("rden", [P, 2, 4])

        region = ExitStack()
        hid = region.enter_context(nc.sbuf_tensor("hid", [P, 32, 2, TOK], F32R))
        mres = region.enter_context(nc.sbuf_tensor("mres", [P, KT, TOK], F32))
        region.close()
        region0 = ExitStack()
        u = region0.enter_context(nc.sbuf_tensor("u", [P, KT, TOK + 2], F32))
        cv = region0.enter_context(nc.sbuf_tensor("cv", [P, KT, TOK], F32))
        region0.close()
        region1 = ExitStack()
        sb1 = lambda n, s: region1.enter_context(nc.sbuf_tensor(n, s, F32))
        qkv = sb1("qkv", [P, 12, TOK])
        kstd = sb1("kstd", [P, 2, TOK])
        kinv = sb1("kinv", [P, 2, TOK])
        vtok = sb1("vtok", [P, 2, TOK])
        sc1 = sb1("sc1", [P, 2, 2, 3 * P])
        pr1 = sb1("pr1", [P, 2, 2, 3 * P])
        pt1 = sb1("pt1", [P, 2, 3 * P])
        qstd = sb1("qstd", [P, 32])
        rq = sb1("rq", [P, 32])
        sb1("unused1", [P, 22 * 2 * TOK - (12 + 2 + 2 + 2) * TOK - 2 * 2 * 2 * 384 - 2 * 384 - 64])
        bias = sb1("bias", [P, HEADS1, 3 * P])
        region1.close()
        region2 = ExitStack()
        sb2 = lambda n, s: region2.enter_context(nc.sbuf_tensor(n, s, F32))
        q2 = sb2("q2", [P, HEADS2, TOK])
        k2 = sb2("k2", [P, HEADS2, TOK])
        vfm = sb2("vfm", [P, 2, TOK])
        vtok2 = sb2("vtok2", [P, 2, D])
        xl = sb2("xl", [P, KT, TOK + 3])
        xc = sb2("xc", [P, KT, TOK])
        rr = sb2("rr", [P, KT, TOK])
        g2 = sb2("g2", [P, KT, TOK])
        ga = sb2("ga", [P, KT, TOK])
        gl = sb2("gl", [P, KT, TOK])
        sc2 = sb2("sc2", [P, 2, 3 * P])
        pr2 = sb2("pr2", [P, 2, 3 * P])
        pt2 = sb2("pt2", [P, 2, 3 * P])
        region2.close()
        mix = q2

        bank = [ctx.enter_context(nc.psum_tensor(f"bank{i}", [P, 512], F32)) for i in range(8)]
        STAT, ATT, OUT = 4, 5, 7

        con = lambda name, n, rows=P: cons[0:rows, CON[name]:CON[name] + n]
        vec = lambda name, i: vecs[:, VEC[name] + i:VEC[name] + i + 1]

        small_in = sem("small_in")
        vecs_loaded = sem("vecs_loaded")
        x_loaded = [sem("x_loaded0"), sem("x_loaded1")]
        first_raw = sem("first_raw")
        raw_loaded = [sem("raw_loaded0"), sem("raw_loaded1")]
        hi_ready = sem("hi_ready")
        lo_ready = sem("lo_ready")
        piece_done = sem("piece_done")
        spilled = sem("spilled")
        summed = sem("summed")
        scaled = sem("scaled")
        split_hi = sem("split_hi")
        split_lo = sem("split_lo")
        resid = sem("resid")
        squared = sem("squared")
        sq_added = sem("sq_added")
        stat_ready = sem("stat_ready")
        rstd_ready = sem("rstd_ready")
        rbc_ready = sem("rbc_ready")
        pad_ready = sem("pad_ready")
        u_ready = sem("u_ready")
        tap_ready = sem("tap_ready")
        conv_step = sem("conv_step")
        cv_ready = sem("cv_ready")
        cy_ready = sem("cy_ready")
        silu_ready = sem("silu_ready")
        gate_ready = sem("gate_ready")
        hval_ready = sem("hval_ready")
        kgain_ready = sem("kgain_ready")
        nsinks_ready = sem("nsinks_ready")
        bias_in = sem("bias_in")
        head_sq = sem("head_sq")
        head_stat = sem("head_stat")
        head_std = sem("head_std")
        head_inv = sem("head_inv")
        k_ready = sem("k_ready")
        v_turned = sem("v_turned")
        v_ready = sem("v_ready")
        scores = sem("scores")
        masked = sem("masked")
        maxed = sem("maxed")
        nmx_ready = sem("nmx_ready")
        negmax = sem("negmax")
        exped = sem("exped")
        den_step = sem("den_step")
        normed = sem("normed")
        probs = sem("probs")
        pt_turned = sem("pt_turned")
        pt_ready = sem("pt_ready")
        att_out = sem("att_out")
        att_hi = sem("att_hi")
        att_lo = sem("att_lo")
        pad2_ready = sem("pad2_ready")
        lam_step = sem("lam_step")
        lam_act = sem("lam_act")
        rot_done = sem("rot_done")
        rot_cos = sem("rot_cos")
        rot_out = sem("rot_out")
        rot_prod = sem("rot_prod")
        pool_scaled = sem("pool_scaled")
        a2_ready = sem("a2_ready")
        roped = sem("roped")
        v2_turned = sem("v2_turned")
        v2_ready = sem("v2_ready")
        tap0 = sem("tap0")
        taps = sem("taps")
        xc_hi = sem("xc_hi")
        xc_lo = sem("xc_lo")
        r_ready = sem("r_ready")
        i_ready = sem("i_ready")
        ix_ready = sem("ix_ready")
        a_ready = sem("a_ready")
        m_step = sem("m_step")
        mult_ready = sem("mult_ready")
        bx_ready = sem("bx_ready")
        scanned = sem("scanned")
        gelu_ready = sem("gelu_ready")
        lru_ready = sem("lru_ready")
        lru_hi = sem("lru_hi")
        lru_lo = sem("lru_lo")
        gates_ready = sem("gates_ready")
        gated_att = sem("gated_att")
        merge_step = sem("merge_step")
        mrg_hi = sem("mrg_hi")
        mrg_lo = sem("mrg_lo")
        post_step = sem("post_step")
        rbc2_ready = sem("rbc2_ready")
        relu_ready = sem("relu_ready")
        sqrelu_ready = sem("sqrelu_ready")
        final = sem("final")
        stored = sem("stored")

        SPLIT = {"mix0": 0, "cy": 8, "ffn0": 16, "hid0": 24, "mix1": 46, "ffn1": 54, "hid1": 62, "pre2": 84,
                 "mpre": 92, "hid2": 100}
        SCALED = {"bx": 0, "up0": 16, "qkv": 38, "up1": 50, "x2": 72, "q2": 80, "k2": 88}
        POOL_SCALED = {"v2": 0, "g2": 8, "ga": 16, "gl": 24}
        NORM = {"mix0": 0, "ffn0": 1, "mix1": 2, "ffn1": 3, "pre2": 4, "post2": 5, "mpre": 6, "mpost": 7}
        RESID = {1: 0, 2: 8, 3: 16, 4: 24, 6: 32}
        R0 = 4 * B0["x2"]
        AT = {name: 4 * B0[name] - R0 for name in ("x2", "q2", "k2", "rg", "v2", "g2", "ga", "gl", "ba")}
        CONV_AT = AT["q2"] - 4
        HEAD_AT = AT["v2"] + 5
        DST = {"x2": xl, "q2": q2, "k2": k2, "g2": g2, "ga": ga, "gl": gl}

        def segment_of(r):
            return [name for name in AT if AT[name] <= r][-1]

        def head_of(r):
            i, odd = divmod(r - HEAD_AT, 3)
            return i if not odd and 0 <= i < HEADS2 else None

        def repeat(eng, count, body):
            if count >= 3:
                with eng.Fori(0, count) as i:
                    body(i)
            else:
                for i in range(count):
                    body(i)

        block = ctx.enter_context(nc.Block())

        @block.sync
        def _(sp):
            sp.dma_start(vecs[:], vecs_in).then_inc(vecs_loaded, 16)
            sp.dma_start(x[:, 0:4, :], x_in[:, 0:4, :]).then_inc(x_loaded[0], 16)
            sp.dma_start(raw[:, 0, 0:PIECE], stream[0:2 * P * PIECE].rearrange("(p n) -> p n", p=P)[:, 0:PIECE])\
              .then_inc(first_raw, 16)
            sp.dma_start(x[:, 4:8, :], x_in[:, 4:8, :]).then_inc(x_loaded[1], 16)
            sp.dma_start(raw[:, 0, PIECE:2 * PIECE],
                         stream[0:2 * P * PIECE].rearrange("(p n) -> p n", p=P)[:, PIECE:2 * PIECE])\
              .then_inc(raw_loaded[0], 16)
            sp.dma_start(cons[:], cons_in).then_inc(small_in, 16)

            def load(b, h, offset, size, waits):
                if waits:
                    if h == 1:
                        sp.wait_ge(lo_ready, 4 * b - 4)
                    sp.wait_ge(raw_loaded[h], 16 * b)
                    if h == 0:
                        sp.wait_ge(lo_ready, 4 * b - 6)
                    sp.wait_ge(x_loaded[1], 16)
                src = stream[bass.ds(offset, P * size)].rearrange("(p n) -> p n", p=P)
                sp.dma_start(raw[:, (b % 2) * 2 + h, 0:size], src).then_inc(raw_loaded[h], 16)

            def loads(first, count):
                def body(i):
                    for h in range(2):
                        load(first + i, h, chunk_offset(2 * first) + (2 * i + h) * 2 * P * PIECE, 2 * PIECE, True)
                repeat(sp, count, body)

            load(0, 1, chunk_offset(1), 2 * PIECE, False)
            sp.dma_start(sinks[:], sinks_in).then_inc(small_in, 16)
            for h in range(2):
                sp.wait_ge(raw_loaded[h], 16)
                load(1, h, chunk_offset(2 + h), 2 * PIECE, False)
            loads(2, 5)
            sp.dma_start(bias[:].rearrange("p h k -> p (h k)"), bias_in_dram).then_inc(bias_in, 16)
            loads(7, B0["dn0"] - 7)
            for name, after in (("dn0", "qkv"), ("dn1", "x2")):
                for c in range(12):
                    load(B0[name] + c // 2, c % 2, chunk_offset(2 * B0[name] + c), 2 * GROUP_K[c % 3][1] * P, True)
                if after == "qkv":
                    loads(B0["qkv"], B0["dn1"] - B0["qkv"])
            loads(B0["x2"], ALL_BODIES - B0["x2"])
            for t in range(KT):
                sp.wait_ge(final, t + 1)
                sp.dma_start(out[:, t, :], x[:, t, :]).then_inc(stored, 16)
            sp.wait_ge(stored, 16 * KT)

        @block.tensor
        def _(pe):
            def blocks(slot, X, tiles, dst, first, last, at=0):
                for i, k in enumerate(tiles):
                    pe.matmul(dst[:, :], whi[:, slot, at + i, :], X[:, k, :, :],
                              start=first and i == 0, stop=False)
                    ins = pe.matmul(dst[:, 0:TOK], wlo[:, slot, at + i, :], X[:, k, 0, :],
                                    start=False, stop=last and i == len(tiles) - 1)
                return ins

            def segment(name, X, split, extra=None):
                count = dict(BODIES)[name]

                def body(i):
                    for p in range(4):
                        n = 4 * (B0[name] + i) + p
                        tile = T0[name] + 4 * i + p
                        pe.wait_ge(lo_ready, n + 1)
                        if T0[name] >= 4:
                            pe.wait_ge(summed, tile - 3)
                        elif isinstance(i, int) and tile >= 4:
                            pe.wait_ge(summed, tile - 3)
                        blocks(p, X, range(8), bank[p], True, True).then_inc(piece_done, 1)
                        if extra:
                            extra(4 * i + p)
                split()
                if extra:
                    for i in range(count):
                        body(i)
                else:
                    repeat(pe, count, body)

            def stat(norm):
                if norm == 0:
                    pe.wait_ge(small_in, 32)
                pe.wait_ge(sq_added, 7 * norm + 7)
                pe.matmul(bank[STAT][:, 0:TOK], con("ones", P), ssum[:], start=True, stop=True)\
                  .then_inc(stat_ready, 1)

            def first_body(name, X, norm, split, split_at, order):
                seen = 0
                for step in order:
                    if step == "norm":
                        if norm is not None:
                            stat(norm)
                        continue
                    a, b, p = step
                    n, tile = 4 * B0[name] + p, T0[name] + p
                    if a == 0:
                        pe.wait_ge(lo_ready, n + 1)
                        if tile >= 4:
                            pe.wait_ge(summed, tile - 3)
                    for k in range(a, b):
                        if k >= seen:
                            pe.wait_ge(split, split_at + k + 1)
                            seen = k + 1
                        ins = blocks(p, X, [k], bank[p], k == 0, k == KT - 1, at=k)
                    if b == KT:
                        ins.then_inc(piece_done, 1)

            STAIR = [(0, 6, 0), (0, 5, 1), (0, 4, 2), "norm", (0, 3, 3), (6, 8, 0), (5, 8, 1), (4, 8, 2), (3, 8, 3)]
            ONE_BY_ONE = [(k, k + 1, p) for k in range(KT - 2) for p in range(4)] + ["norm"] \
                + [(KT - 2, KT, p) for p in range(4)]
            IN_ORDER = [(0, 8, 0), "norm", (0, 8, 1), (0, 8, 2), (0, 8, 3)]

            def rest(name, X, extra=None):
                count = dict(BODIES)[name] - 1

                def body(i):
                    for p in range(4):
                        pe.wait_ge(lo_ready, 4 * (B0[name] + 1 + i) + p + 1)
                        pe.wait_ge(summed, T0[name] + 4 * (1 + i) + p - 3)
                        blocks(p, X, range(8), bank[p], True, True).then_inc(piece_done, 1)
                        if extra:
                            extra(4 * (1 + i) + p)
                if extra:
                    for i in range(count):
                        body(i)
                else:
                    repeat(pe, count, body)

            def gated_down(name, split_at):
                for q in range(24):
                    g, c, m = q // 6, q // 2 % 3, q % 2
                    k0, kts = GROUP_K[c]
                    n, tile = 4 * B0[name] + q, T0[name] + 2 * g + m
                    pe.wait_ge(lo_ready, n + 1)
                    if q == 0:
                        pe.wait_ge(split_lo, split_at + 20)
                    if q == 4:
                        pe.wait_ge(split_lo, split_at + FT)
                    if c == 0:
                        pe.wait_ge(summed, tile - 3)
                    blocks(n % 4, hid, range(k0, k0 + kts), bank[tile % 4], c == 0, c == 2)\
                        .then_inc(piece_done, 1)

            first_body("bx", xa, NORM["mix0"], split_lo, SPLIT["mix0"], IN_ORDER)
            rest("bx", xa)
            def c_tiles():
                for i in range(8):
                    pe.wait_ge(lo_ready, 4 * B0["c"] + i + 1)
                    pe.wait_ge(summed, T0["c"] + i - 3)
                    blocks(i % 4, xa, range(8), bank[i % 4], True, True).then_inc(piece_done, 1)
            c_tiles()
            first_body("o", xb, None, split_lo, SPLIT["cy"], STAIR)
            rest("o", xb)
            first_body("up0", xa, NORM["ffn0"], split_lo, SPLIT["ffn0"], STAIR)
            rest("up0", xa)
            gated_down("dn0", SPLIT["hid0"])

            def head_sums(i):
                t = i - 1
                if 0 <= t < 2:
                    pe.wait_ge(head_sq, t + 1)
                    pe.matmul(bank[ATT + t][:, 0:TOK], con("half", P), sq[:, t, :],
                              start=True, stop=True).then_inc(head_stat, 1)
                if 4 <= t < 12:
                    pe.wait_ge(head_sq, t - 1)
                    for tb in range(2):
                        at = TOK + 4 * (t - 4) + 2 * tb
                        ins = pe.matmul(bank[STAT][:, at:at + 2], sq[:, t % 2, tb * P:(tb + 1) * P],
                                        con("half", P)[:, 0:P:P // 2], start=True, stop=True)
                    ins.then_inc(head_stat, 1)
            first_body("qkv", xa, NORM["mix1"], split_lo, SPLIT["mix1"], STAIR)
            for i in range(4, 12):
                pe.wait_ge(lo_ready, 4 * B0["qkv"] + i + 1)
                pe.wait_ge(summed, T0["qkv"] + i - 3)
                blocks(i % 4, xa, range(8), bank[i % 4], True, True).then_inc(piece_done, 1)
                if i < 6:
                    head_sums(i - 3)
                if i == 6:
                    pe.wait_ge(scaled, SCALED["qkv"] + 4)
                    for f in range(2):
                        for tb in range(2):
                            ins = pe.transpose(bank[OUT][:, (2 * tb + f) * P:(2 * tb + f + 1) * P],
                                               qkv[:, 2 + f, tb * P:(tb + 1) * P], con("ident", P))
                    ins.then_inc(v_turned, 1)
                head_sums(i if i >= 5 else 0)
            head_sums(12)

            def scores1(i):
                if i >= 2:
                    pe.wait_ge(masked, i - 1)
                for h in range(2):
                    b = bank[2 * (i % 2) + h]
                    q = qkv[64 * h:64 * h + 64, 4 + i, :]
                    k = qkv[64 * h:64 * h + 64, i // 4, :]
                    pe.matmul(b[:, 0:P], q[:, 0:P], k[:, 0:P], start=True, stop=True)
                    ins = pe.matmul(b[:, P:3 * P], q[:, P:2 * P], k[:, :], start=True, stop=True)
                ins.then_inc(scores, 1)

            def turn1(i):
                pe.wait_ge(normed, i + 1)
                if i >= 1:
                    pe.wait_ge(pt_ready, i)
                for h in range(2):
                    for j in range(3):
                        ins = pe.transpose(bank[ATT + h][:, j * P:(j + 1) * P], pr1[:, i % 2, h, j * P:(j + 1) * P],
                                           con("ident", P))
                ins.then_inc(pt_turned, 1)

            def values1(i):
                pe.wait_ge(pt_ready, i + 1)
                if i >= 2:
                    pe.wait_ge(att_lo, i - 1)
                for h in range(2):
                    o = bank[STAT if i % 2 == 0 else OUT][64 * h:64 * h + 64, :]
                    g = 2 * (i // 4) + h
                    v = [vtok[:, tb, g * 64:g * 64 + 64] for tb in range(2)]
                    pt = pt1[:, h, :]
                    pe.matmul(o[:, 0:P], v[0], pt[:, 0:P], start=True, stop=True)
                    pe.matmul(o[:, P:2 * P], v[0], pt[:, P:2 * P], start=True, stop=False)
                    ins = pe.matmul(o[:, P:2 * P], v[1], pt[:, 2 * P:3 * P], start=False, stop=True)
                ins.then_inc(att_out, 1)

            pe.wait_ge(summed, T0["qkv"] + 12)
            pe.wait_ge(scaled, SCALED["qkv"] + 12)
            pe.wait_ge(k_ready, 2)
            pe.wait_ge(v_ready, 1)
            scores1(0)
            for s in range(PAIRS1 + 2):
                if s >= 2:
                    turn1(s - 2)
                if s + 1 < PAIRS1:
                    scores1(s + 1)
                if s == 2:
                    pe.wait_ge(head_inv, 3)
                if s >= 2:
                    values1(s - 2)

            first_body("wo", xb, None, att_lo, 0, STAIR)
            rest("wo", xb)
            first_body("up1", xa, NORM["ffn1"], split_lo, SPLIT["ffn1"], STAIR)
            rest("up1", xa)
            gated_down("dn1", SPLIT["hid1"])

            def rotate(j):
                src, t = (q2, j) if j < 8 else (k2, j - 8)
                pe.wait_ge(scaled, SCALED["q2" if j < 8 else "k2"] + t + 1)
                if j >= 2:
                    pe.wait_ge(rot_out, j - 1)
                pe.matmul(bank[ATT + j % 2][0:ROT, 0:TOK], con("rot", ROT, ROT), src[0:ROT, t, :],
                          start=True, stop=True).then_inc(rot_done, 1)

            def turn_v(t):
                pe.wait_ge(pool_scaled, t + 1)
                if t >= 1:
                    pe.wait_ge(v2_ready, t)
                for tb in range(2):
                    ins = pe.transpose(bank[STAT][:, tb * P:(tb + 1) * P], vfm[:, t % 2, tb * P:(tb + 1) * P],
                                       con("ident", P))
                ins.then_inc(v2_turned, 1)

            def scores2(i):
                h = PAIRS1 + i
                pe.wait_ge(roped, 8 + i + 1)
                if i >= 2:
                    pe.wait_ge(masked, h - 1)
                b = bank[ATT + i % 2]
                pe.matmul(b[:, 0:P], q2[:, i, 0:P], k2[:, i, 0:P], start=True, stop=True)
                pe.matmul(b[:, P:3 * P], q2[:, i, P:2 * P], k2[:, i, :], start=True, stop=True)\
                  .then_inc(scores, 1)

            def turn2(i):
                h = PAIRS1 + i
                pe.wait_ge(probs, i + 1)
                if i >= 1:
                    pe.wait_ge(pt_ready, h)
                else:
                    pe.wait_ge(v2_ready, 8)
                for j in range(3):
                    ins = pe.transpose(bank[STAT][:, j * P:(j + 1) * P], pr2[:, i % 2, j * P:(j + 1) * P],
                                       con("ident", P))
                ins.then_inc(pt_turned, 1)

            def values2(i):
                h = PAIRS1 + i
                pe.wait_ge(pt_ready, h + 1)
                if i >= 1:
                    pe.wait_ge(att_lo, h)
                o = bank[OUT]
                v = [vtok2[:, tb, i * HD2:(i + 1) * HD2] for tb in range(2)]
                pt = pt2[:, i % 2, :]
                pe.matmul(o[:, 0:P], v[0], pt[:, 0:P], start=True, stop=True)
                pe.matmul(o[:, P:2 * P], v[0], pt[:, P:2 * P], start=True, stop=False)
                pe.matmul(o[:, P:2 * P], v[1], pt[:, 2 * P:3 * P], start=False, stop=True).then_inc(att_out, 1)

            def beside(r):
                if 0 <= r - AT["q2"] - 1 < 8:
                    rotate(r - AT["q2"] - 1)
                if 0 <= r - AT["k2"] - 1 < 8:
                    rotate(8 + r - AT["k2"] - 1)
                if 0 <= r - AT["v2"] - 1 < 8:
                    turn_v(r - AT["v2"] - 1)
                if head_of(r) is not None:
                    scores2(head_of(r))
                if head_of(r - 4) is not None:
                    turn2(head_of(r - 4))
                if head_of(r - 5) is not None:
                    values2(head_of(r - 5))

            first_body("x2", xa, NORM["pre2"], split_lo, SPLIT["pre2"], STAIR)
            for r in range(4, AT["ba"]):
                n = R0 + r
                pe.wait_ge(lo_ready, n + 1)
                if AT["rg"] <= r < AT["v2"]:
                    part = r - AT["rg"]
                    if part < 2:
                        pe.wait_ge(xc_lo, 4 * part + 4)
                    for m in range(4):
                        tile, t = T0["rg"] + 4 * part + m, 4 * (part % 2) + m
                        pe.wait_ge(summed, tile - 3)
                        ins = blocks(r % 4, xb, [t // 2 * 2, t // 2 * 2 + 1], bank[m], True, True, at=2 * m)
                    ins.then_inc(piece_done, 1)
                else:
                    tile = T0[segment_of(r)] + r - AT[segment_of(r)]
                    pe.wait_ge(summed, tile - 3)
                    blocks(r % 4, xa, range(8), bank[r % 4], True, True).then_inc(piece_done, 1)
                beside(r)

            first_body("ba", xb, None, att_lo, PAIRS1, STAIR)
            rest("ba", xb)
            first_body("bl", xa, None, lru_lo, 0, STAIR)
            rest("bl", xa)
            first_body("out2", xb, None, mrg_lo, 0, STAIR)
            rest("out2", xb)
            stat(NORM["post2"])
            first_body("mup", xa, NORM["mpre"], split_lo, SPLIT["mpre"], ONE_BY_ONE)
            rest("mup", xa)
            for q in range(32):
                g, c, m = q // 8, q // 2 % 4, q % 2
                n, tile = 4 * B0["mdn"] + q, T0["mdn"] + 2 * g + m
                pe.wait_ge(lo_ready, n + 1)
                if q in (0, 6):
                    pe.wait_ge(split_lo, SPLIT["hid2"] + (24 if q == 0 else 32))
                if c == 0:
                    pe.wait_ge(summed, tile - 3)
                blocks(n % 4, hid, range(8 * c, 8 * c + 8), bank[tile % 4], c == 0, c == 3)\
                    .then_inc(piece_done, 1)
            stat(NORM["mpost"])

        @block.scalar
        def _(act):
            def round_weights(b, p, kts=8, free=True):
                if p % 2 == 0 and (free or p > 0):
                    act.wait_ge(raw_loaded[p // 2], 16 * b + 16)
                if not free and p == 1:
                    act.wait_ge(raw_loaded[0], 16)
                if free:
                    act.wait_ge(piece_done, 4 * b + p - 3)
                slot = (b % 2) * 2 + p // 2
                src = raw[:, slot, (p % 2) * kts * P:(p % 2 + 1) * kts * P]
                act.activation(whi[:, p, 0:kts, :].rearrange("p k m -> p (k m)"), src, ACT.Copy)\
                   .then_inc(hi_ready, 1)

            def next_weights(n):
                if n + 4 < 4 * ALL_BODIES:
                    round_weights((n + 4) // 4, n % 4, blocks_of(n + 4))

            def spill_tile(n, tile, slot):
                act.wait_ge(piece_done, n + 1)
                if not isinstance(tile, int) or tile >= 4:
                    act.wait_ge(summed, tile - 3)
                act.activation(spill[:, slot, :], bank[slot][:, TOK:2 * TOK], ACT.Copy).then_inc(spilled, 1)

            def square(t, norm, src):
                if t >= 2:
                    act.wait_ge(sq_added, 7 * norm + max(1, t - 2))
                elif norm > 0:
                    act.wait_ge(sq_added, 7 * norm)
                act.activation(sq[:, t % 2, :], src, ACT.Square).then_inc(squared, 1)

            def norm_tile(t, gain, norm, split_at):
                if norm > 0:
                    act.wait_ge(resid, RESID[norm] + t + 1)
                act.activation(xa[:, t, 0, :], x[:, t, :], ACT.Copy, scale=vec(gain, t)).then_inc(split_hi, 1)
                square(t, norm, x[:, t, :])

            def rms(norm):
                act.wait_ge(stat_ready, norm + 1)
                act.activation(rstd[:], bank[STAT][:, 0:TOK], ACT.Sqrt, scale=1.0 / D, bias=EPS)\
                   .then_inc(rstd_ready, 1)

            act.wait_ge(vecs_loaded, 16)
            for t in range(KT):
                if t % 4 == 0:
                    act.wait_ge(x_loaded[t // 4], 16)
                act.activation(xa[:, t, 0, :], x[:, t, :], ACT.Copy, scale=vec("mix0", t)).then_inc(split_hi, 1)
                if t == 1:
                    act.wait_ge(first_raw, 16)
                if t % 2 == 1:
                    round_weights(0, t // 2, free=False)
                    for k in (t - 1, t):
                        square(k, 0, x[:, k, :])

            def decay_constant(q):
                if q == 1:
                    act.wait_ge(lam_step, 2)
                    act.activation(lamb[:, 1, :], lamb[:, 0, :], ACT.Exp, scale=-1.0).then_inc(lam_act, 1)
                if q == 3:
                    act.wait_ge(lam_step, 3)
                    act.activation(lamb[:, 3, :], lamb[:, 2, :], ACT.Ln).then_inc(lam_act, 1)

            def first_tap(t):
                act.wait_ge(u_ready, t + 1)
                act.activation(cv[:, t, :], u[:, t, 0:TOK], ACT.Copy, scale=vec("conv", t)).then_inc(tap_ready, 1)

            def bx_step(i, p):
                n = 4 * (B0["bx"] + i) + p
                spill_tile(n, T0["bx"] + 4 * i + p, p)
                if isinstance(i, int) and i == 0 and p == 0:
                    rms(0)
                round_weights(B0["bx"] + i + 1, p)
            for i in range(4):
                for p in range(4):
                    bx_step(i, p)
                    if i >= 1 and p % 2 == 1:
                        first_tap(2 * i - 2 + p // 2)

            for t in range(8):
                n = 4 * B0["c"] + t
                spill_tile(n, T0["c"] + t, t % 4)
                next_weights(n)
                if t < 2:
                    first_tap(6 + t)
                act.wait_ge(cy_ready, t + 1)
                act.activation(xb[:, t, 0, :], z[:, t % 4, :], ACT.Copy).then_inc(split_hi, 1)

            def residual_part(name, gain, norm, split_at):
                for t in range(8):
                    n = 4 * B0[name] + t
                    spill_tile(n, T0[name] + t, t % 4)
                    next_weights(n)
                    norm_tile(t, gain, norm, split_at)

            def gated_up(name, norm, layer):
                base = 22 * layer

                def body(i):
                    for p in range(4):
                        n = 4 * (B0[name] + i) + p
                        if isinstance(i, int) and i == 0 and p == 0:
                            rms(norm)
                        spill_tile(n, T0[name] + 4 * i + p, p)
                        round_weights(B0[name] + i + 1, p)
                        if p < 2:
                            act.wait_ge(scaled, SCALED[name] + 2 * i + p + 1)
                            act.wait_ge(gate_ready, base + 2 * i)
                            act.activation(act1[:, p, :], z[:, p, :], ACT.Silu).then_inc(silu_ready, 1)
                        else:
                            act.wait_ge(hval_ready, base + 2 * i + p - 1)
                            act.activation(hid[:, 2 * i + p - 2, 0, :], z[:, p, :], ACT.Copy).then_inc(split_hi, 1)
                body(0)
                repeat(act, 10, lambda i: body(i + 1))

            def gated_down(name, gain, norm, split_at):
                for q in range(24):
                    n = 4 * B0[name] + q
                    g, c, m = q // 6, q // 2 % 3, q % 2
                    t = 2 * g + m
                    if c == 2:
                        spill_tile(n, T0[name] + t, (T0[name] + t) % 4)
                    next_weights(n)
                    if name == "dn0":
                        decay_constant(q)
                    if c == 2:
                        norm_tile(t, gain, norm, split_at)

            residual_part("o", "ffn0", NORM["ffn0"], SPLIT["ffn0"])
            gated_up("up0", NORM["ffn0"], 0)
            gated_down("dn0", "mix1", NORM["mix1"], SPLIT["mix1"])

            for t in range(12):
                n = 4 * B0["qkv"] + t
                if t == 0:
                    rms(NORM["mix1"])
                spill_tile(n, T0["qkv"] + t, t % 4)
                next_weights(n)
                if t not in (2, 3):
                    j = t if t < 2 else t - 2
                    act.wait_ge(scaled, SCALED["qkv"] + t + 1)
                    if j >= 2:
                        act.wait_ge(head_stat, j - 1)
                    else:
                        act.wait_ge(sq_added, 7 * NORM["mix1"] + 7)
                    act.activation(sq[:, t % 2, :], qkv[:, t, :], ACT.Square).then_inc(head_sq, 1)
                if t == 6:
                    for j in range(2):
                        act.wait_ge(head_stat, j + 1)
                        act.activation(kstd[:, j, :], bank[ATT + j][:, 0:TOK], ACT.Sqrt, scale=1.0 / HD1, bias=EPS)\
                           .then_inc(head_std, 1)
                if t == 7:
                    act.wait_ge(v_turned, 1)
                    act.activation(vtok[:].rearrange("p a b -> p (a b)"), bank[OUT][:, :], ACT.Copy)\
                       .then_inc(v_ready, 1)
            act.wait_ge(head_stat, 10)
            act.activation(qstd[:], bank[STAT][:, TOK:TOK + 32], ACT.Sqrt, scale=1.0 / HD1, bias=EPS)\
               .then_inc(head_std, 1)

            def exps1(i):
                s = i % 2
                if i >= 2:
                    act.wait_ge(pt_turned, i - 1)
                act.wait_ge(negmax, i + 1)
                for b in range(2):
                    cols = slice(0, P) if b == 0 else slice(P, 3 * P)
                    for h in range(2):
                        j = 2 * b + h
                        act.activation(pr1[:, s, h, cols], sc1[:, s, h, cols], ACT.Exp, bias=nmx[:, s, j:j + 1],
                                       accum_out=den[:, s, j:j + 1])
                act.activation(esink[:, s, :], mx[:, s, :], ACT.Exp).then_inc(exped, 1)

            def copy_turned1(i):
                act.wait_ge(pt_turned, i + 1)
                if i >= 1:
                    act.wait_ge(att_out, i)
                for h in range(2):
                    ins = act.activation(pt1[:, h, :], bank[ATT + h][:, 0:3 * P], ACT.Copy)
                ins.then_inc(pt_ready, 1)

            for s in range(PAIRS1 + 3):
                if 2 <= s <= PAIRS1 + 1:
                    copy_turned1(s - 2)
                if s >= 3:
                    i = s - 3
                    act.wait_ge(att_out, i + 1)
                    act.activation(xb[:, i, 0, :], bank[STAT if i % 2 == 0 else OUT][:, 0:TOK], ACT.Copy)\
                       .then_inc(att_hi, 1)
                if s < PAIRS1:
                    exps1(s)

            def exps(i, sc, pr):
                h, s = PAIRS1 + i, i % 2
                act.wait_ge(negmax, h + 1)
                if i >= 2:
                    act.wait_ge(pt_turned, h - 1)
                act.activation(pr[:, s, 0:P], sc[:, s, 0:P], ACT.Exp, bias=nmx[:, s, 0:1],
                               accum_out=den[:, s, 0:1])
                act.activation(pr[:, s, P:3 * P], sc[:, s, P:3 * P], ACT.Exp, bias=nmx[:, s, 1:2],
                               accum_out=den[:, s, 1:2]).then_inc(exped, 1)

            def copy_turned(i, pt):
                h = PAIRS1 + i
                act.wait_ge(pt_turned, h + 1)
                if i >= 2:
                    act.wait_ge(att_out, h - 1)
                act.activation(pt[:, i % 2, :], bank[STAT][:, 0:3 * P], ACT.Copy).then_inc(pt_ready, 1)

            residual_part("wo", "ffn1", NORM["ffn1"], SPLIT["ffn1"])
            gated_up("up1", NORM["ffn1"], 1)
            gated_down("dn1", "pre2", NORM["pre2"], SPLIT["pre2"])

            def beside(r):
                if 0 <= r - CONV_AT < 16:
                    t = (r - CONV_AT) // 2
                    if r % 2 == 0:
                        act.wait_ge(scaled, SCALED["x2"] + t + 1)
                        act.wait_ge(pad2_ready, 1)
                        act.activation(xc[:, t, :], xl[:, t, 0:TOK], ACT.Identity, scale=vec("conv2", t),
                                       bias=vec("convb2", t)).then_inc(tap0, 1)
                    if r % 2 == 0 and t >= 1:
                        act.wait_ge(taps, 3 * t)
                        act.activation(xb[:, t - 1, 0, :], xc[:, t - 1, :], ACT.Copy).then_inc(xc_hi, 1)
                if r == CONV_AT + 16:
                    act.wait_ge(taps, 24)
                    act.activation(xb[:, 7, 0, :], xc[:, 7, :], ACT.Copy).then_inc(xc_hi, 1)
                for first, at in ((0, AT["q2"] + 2), (8, AT["k2"] + 2)):
                    if 0 <= r - at < 8:
                        j = first + r - at
                        act.wait_ge(rot_done, j + 1)
                        if j >= 2:
                            act.wait_ge(roped, j - 1)
                        act.activation(rtmp[:, j % 2, 1, :], bank[ATT + j % 2][0:ROT, 0:TOK], ACT.Copy)\
                           .then_inc(rot_out, 1)
                if 0 <= r - AT["v2"] < 16:
                    t, odd = divmod(r - AT["v2"], 2)
                    if not odd:
                        if t == 0:
                            act.wait_ge(lam_step, 10)
                        if t >= 2:
                            act.wait_ge(m_step, t - 1)
                        act.activation(gate[:, t % 2, :], rr[:, t, :], ACT.Tanh, scale=lam8[:, t:t + 1])
                        act.activation(rr[:, t, :], rr[:, t, :], ACT.Exp, scale=nlam8[:, t:t + 1]).then_inc(a_ready, 1)
                    else:
                        act.wait_ge(a_ready, t + 1)
                        act.activation(sq[:, t % 2, :], rr[:, t, :], ACT.Square).then_inc(a2_ready, 1)
                if r == AT["v2"] + 17:
                    act.wait_ge(m_step, KT)
                    act.activation(xl[:, :, 0:TOK], xl[:, :, 0:TOK], ACT.Sqrt).then_inc(mult_ready, 1)
                if head_of(r - 5) is not None:
                    i = head_of(r - 5)
                    act.wait_ge(att_out, PAIRS1 + i + 1)
                    act.activation(xb[:, i, 0, :], bank[OUT][:, 0:TOK], ACT.Copy).then_inc(att_hi, 1)
                if head_of(r - 1) is not None:
                    exps(head_of(r - 1), sc2, pr2)
                if head_of(r - 4) is not None:
                    copy_turned(head_of(r - 4), pt2)
                if r == AT["v2"] + 19:
                    act.wait_ge(pool_scaled, POOL_SCALED["g2"] + 8)
                    act.activation(g2[:], g2[:], ACT.Gelu_apprx_tanh).then_inc(gelu_ready, 1)
                if r == AT["ba"] - 1:
                    act.wait_ge(pool_scaled, POOL_SCALED["ga"] + 8)
                    act.activation(ga[:], ga[:], ACT.Sigmoid).then_inc(gates_ready, 1)

            for r in range(AT["ba"]):
                n = R0 + r
                if AT["rg"] <= r < AT["v2"]:
                    part = r - AT["rg"]
                    for m in range(4):
                        spill_tile(n, T0["rg"] + 4 * part + m, m)
                    next_weights(n)
                    for m in range(4):
                        t = 4 * (part % 2) + m
                        act.wait_ge(summed, T0["rg"] + 4 * part + m + 1)
                        if part < 2:
                            act.activation(rr[:, t, :], z[:, m, :], ACT.Sigmoid, bias=vec("ba", t)).then_inc(r_ready, 1)
                        else:
                            if t >= 2:
                                act.wait_ge(ix_ready, t - 1)
                            act.activation(act1[:, t % 2, :], z[:, m, :], ACT.Sigmoid, bias=vec("bi", t))\
                               .then_inc(i_ready, 1)
                else:
                    if r == 0:
                        rms(NORM["pre2"])
                    spill_tile(n, T0[segment_of(r)] + r - AT[segment_of(r)], r % 4)
                    if 0 <= r - AT["v2"] - 2 < 8:
                        t = r - AT["v2"] - 2
                        act.wait_ge(v2_turned, t + 1)
                        act.activation(vtok2[:, :, t * P:(t + 1) * P],
                                       bank[STAT][:, 0:TOK].rearrange("p (a b) -> p a b", a=2), ACT.Copy)\
                           .then_inc(v2_ready, 1)
                    next_weights(n)
                beside(r)
            for t in range(8):
                n = 4 * B0["ba"] + t
                spill_tile(n, T0["ba"] + t, t % 4)
                next_weights(n)
                for k in range(t - 1, t if t < 7 else 8):
                    if k >= 0:
                        act.wait_ge(lru_ready, k + 1)
                        act.activation(xa[:, k, 0, :], xc[:, k, :], ACT.Copy).then_inc(lru_hi, 1)
                if t == 1:
                    act.wait_ge(pool_scaled, POOL_SCALED["gl"] + 8)
                    act.activation(gl[:], gl[:], ACT.Sigmoid).then_inc(gates_ready, 1)
            for t in range(8):
                n = 4 * B0["bl"] + t
                spill_tile(n, T0["bl"] + t, t % 4)
                next_weights(n)
                act.wait_ge(merge_step, 2 * t + 2)
                act.activation(xb[:, t, 0, :], z[:, t % 4, :], ACT.Copy).then_inc(mrg_hi, 1)
            for t in range(8):
                n = 4 * B0["out2"] + t
                spill_tile(n, T0["out2"] + t, t % 4)
                next_weights(n)
                act.wait_ge(summed, T0["out2"] + t + 1)
                square(t, NORM["post2"], mix[:, t, :])
            rms(NORM["post2"])
            for t in range(8):
                norm_tile(t, "mpre", NORM["mpre"], SPLIT["mpre"])

            def up_hi(tile, slot):
                act.wait_ge(sqrelu_ready, tile + 1)
                act.activation(hid[:, tile, 0, :], z[:, slot, :], ACT.Copy).then_inc(split_hi, 1)

            def squared_up(i):
                for p in range(4):
                    if isinstance(i, int) and i == 0 and p == 0:
                        rms(NORM["mpre"])
                    spill_tile(4 * (B0["mup"] + i) + p, T0["mup"] + 4 * i + p, p)
                    round_weights(B0["mup"] + i + 1, p)
                    if p > 0 or not isinstance(i, int):
                        up_hi(4 * i + p - 1, (p - 1) % 4)
            squared_up(0)
            repeat(act, 7, lambda i: squared_up(i + 1))
            up_hi(31, 3)
            for q in range(32):
                n = 4 * B0["mdn"] + q
                t = 2 * (q // 8) + q % 2
                if q // 2 % 4 == 3:
                    spill_tile(n, T0["mdn"] + t, (T0["mdn"] + t) % 4)
                next_weights(n)
                if q // 2 % 4 == 3:
                    act.wait_ge(summed, T0["mdn"] + t + 1)
                    square(t, NORM["mpost"], mres[:, t, :])
            rms(NORM["mpost"])

        @block.vector
        def _(dve):
            def rest_weights(b, p, kts=8, free=True):
                dve.wait_ge(hi_ready, 4 * b + p + 1)
                if free:
                    dve.wait_ge(piece_done, 4 * b + p - 3)
                slot = (b % 2) * 2 + p // 2
                src = raw[:, slot, (p % 2) * kts * P:(p % 2 + 1) * kts * P]
                dve.tensor_tensor(wlo[:, p, 0:kts, :].rearrange("p k m -> p (k m)"), src,
                                  whi[:, p, 0:kts, :].rearrange("p k m -> p (k m)").bitcast(F32), ALU.subtract)\
                   .then_inc(lo_ready, 1)

            def next_weights(n):
                if n + 4 < 4 * ALL_BODIES:
                    rest_weights((n + 4) // 4, n % 4, blocks_of(n + 4))

            def sum_tile(tile, slot, dst=None):
                dve.wait_ge(spilled, tile + 1)
                dve.tensor_tensor(z[:, slot, :] if dst is None else dst, bank[slot][:, 0:TOK], spill[:, slot, :], ALU.add)\
                   .then_inc(summed, 1)

            def scale_tile(tile, slot, dst=None):
                dve.wait_ge(summed, tile + 1)
                dve.tensor_tensor(z[:, slot, :] if dst is None else dst, z[:, slot, :], rbc[:], ALU.mult)\
                   .then_inc(scaled, 1)

            def rms(norm):
                dve.wait_ge(rstd_ready, norm + 1)
                dve.reciprocal(rbc[:], rstd[:]).then_inc(rbc_ready, 1)
                dve.wait_ge(rbc_ready, norm + 1)

            def norm_lo(t, gain, split_at):
                dve.wait_ge(split_hi, split_at + t + 1)
                dve.scalar_tensor_tensor(out=xa[:, t, 1, :], in0=x[:, t, :], scalar=vec(gain, t),
                                         in1=xa[:, t, 0, :].bitcast(F32), op0=ALU.mult, op1=ALU.subtract)\
                   .then_inc(split_lo, 1)

            dve.memset(u[:, :, 0:2], 0.0).then_inc(pad_ready, 1)
            dve.wait_ge(vecs_loaded, 16)
            dve.scalar_tensor_tensor(out=kgain[:], in0=vec("qg", 0), scalar=HD1 ** -0.5, in1=vec("kg", 0),
                                     op0=ALU.mult, op1=ALU.mult).then_inc(kgain_ready, 1)
            for t in range(KT):
                if t % 4 == 0:
                    dve.wait_ge(x_loaded[t // 4], 16)
                norm_lo(t, "mix0", SPLIT["mix0"])
                if t % 2 == 1:
                    rest_weights(0, t // 2, free=False)

            def decay_constant(q):
                lam = vecs[:, VEC["lam"]:VEC["lam"] + KT]
                L = [lamb[:, i, :] for i in range(6)]
                if q == 0:
                    dve.tensor_scalar(L[5], lam, -1.0, None, ALU.mult).then_inc(lam_step, 1)
                    dve.wait_ge(lam_step, 1)
                    dve.tensor_tensor(L[0], lam, L[5], ALU.max).then_inc(lam_step, 1)
                if q == 2:
                    dve.wait_ge(lam_act, 1)
                    dve.tensor_scalar(L[2], L[1], 1.0, None, ALU.add).then_inc(lam_step, 1)
                    dve.wait_ge(lam_step, 3)
                    dve.tensor_scalar(L[4], L[2], -1.0, 1e-30, ALU.add, ALU.max).then_inc(lam_step, 1)
                    dve.wait_ge(lam_step, 4)
                    dve.reciprocal(L[0], L[4]).then_inc(lam_step, 1)
                if q == 4:
                    dve.wait_ge(lam_step, 5)
                    dve.wait_ge(lam_act, 2)
                    dve.tensor_tensor(L[4], L[3], L[0], ALU.mult).then_inc(lam_step, 1)
                    dve.wait_ge(lam_step, 6)
                    dve.scalar_tensor_tensor(out=L[4], in0=L[2], scalar=1.0, in1=L[4], op0=ALU.is_equal,
                                             op1=ALU.add).then_inc(lam_step, 1)
                    dve.wait_ge(lam_step, 7)
                    dve.tensor_tensor(L[4], L[4], L[1], ALU.mult).then_inc(lam_step, 1)
                    dve.wait_ge(lam_step, 8)
                    dve.scalar_tensor_tensor(out=L[3], in0=L[5], scalar=0.0, in1=L[4], op0=ALU.max,
                                             op1=ALU.add).then_inc(lam_step, 1)
                    dve.wait_ge(lam_step, 9)
                    dve.tensor_scalar(lam8[:], L[3], 8.0, None, ALU.mult)
                    dve.tensor_scalar(nlam8[:], L[3], -8.0, None, ALU.mult).then_inc(lam_step, 1)
                if q == 5:
                    dve.wait_ge(small_in, 32)
                    dve.tensor_scalar(nsinks[:], sinks[:], -1.0, None, ALU.mult).then_inc(nsinks_ready, 1)

            def bx_step(i, p):
                tile = T0["bx"] + 4 * i + p
                if not isinstance(i, int):
                    dve.wait_ge(u_ready, 2 * i)
                elif i >= 1:
                    dve.wait_ge(u_ready, 2 * i)
                sum_tile(tile, p)
                if isinstance(i, int) and i == 0 and p == 0:
                    rms(0)
                scale_tile(tile, p)
                rest_weights(B0["bx"] + i + 1, p)
            def conv_taps(t0):
                for tap in (1, 2):
                    for t in (t0, t0 + 1):
                        if tap == 1:
                            dve.wait_ge(tap_ready, t + 1)
                        else:
                            dve.wait_ge(conv_step, 2 * t0 + 1 + t - t0)
                        dve.scalar_tensor_tensor(out=cv[:, t, :], in0=u[:, t, tap:TOK + tap],
                                                 scalar=vec("conv", 8 * tap + t), in1=cv[:, t, :],
                                                 op0=ALU.mult, op1=ALU.add).then_inc(conv_step, 1)
            for i in range(4):
                for p in range(4):
                    bx_step(i, p)
                if i >= 1:
                    conv_taps(2 * i - 2)

            def split_lo_z(t):
                dve.wait_ge(cy_ready, t + 1)
                dve.wait_ge(split_hi, SPLIT["cy"] + t + 1)
                dve.tensor_tensor(xb[:, t, 1, :], z[:, t % 4, :], xb[:, t, 0, :].bitcast(F32), ALU.subtract)\
                   .then_inc(split_lo, 1)

            for t in range(8):
                tile = T0["c"] + t
                if t == 0:
                    dve.wait_ge(u_ready, 8)
                sum_tile(tile, t % 4)
                dve.wait_ge(summed, tile + 1)
                dve.wait_ge(cv_ready, t + 1)
                dve.tensor_tensor(z[:, t % 4, :], z[:, t % 4, :], cv[:, t, :], ALU.mult).then_inc(cy_ready, 1)
                next_weights(4 * B0["c"] + t)
                split_lo_z(t)
                if t == 1:
                    conv_taps(6)

            def add_residual(t, tile, norm):
                dve.wait_ge(summed, tile + 1)
                dve.tensor_tensor(x[:, t, :], x[:, t, :], z[:, tile % 4, :], ALU.add).then_inc(resid, 1)

            def residual_part(name, gain, norm, split_at):
                for t in range(8):
                    tile = T0[name] + t
                    sum_tile(tile, tile % 4)
                    add_residual(t, tile, norm)
                    next_weights(4 * B0[name] + t)
                    norm_lo(t, gain, split_at)

            def gated_up(name, norm, layer):
                base = 22 * layer
                split_at = SPLIT["hid0"] if layer == 0 else SPLIT["hid1"]

                def body(i):
                    for p in range(4):
                        tile = T0[name] + 4 * i + p
                        if isinstance(i, int) and i == 0 and p == 0:
                            rms(norm)
                        if p < 2 and not (isinstance(i, int) and base + 2 * i == 0):
                            dve.wait_ge(silu_ready, base + 2 * i)
                        sum_tile(tile, p)
                        if p < 2:
                            scale_tile(tile, p)
                        else:
                            dve.wait_ge(summed, tile + 1)
                            dve.wait_ge(gate_ready, base + 2 * i + p - 1)
                            dve.tensor_tensor(z[:, p, :], z[:, p, :], gate[:, p - 2, :], ALU.mult)\
                               .then_inc(hval_ready, 1)
                        rest_weights(B0[name] + i + 1, p)
                    for m in range(2):
                        dve.wait_ge(split_hi, split_at + 2 * i + m + 1)
                        dve.tensor_tensor(hid[:, 2 * i + m, 1, :], z[:, 2 + m, :],
                                          hid[:, 2 * i + m, 0, :].bitcast(F32), ALU.subtract)\
                           .then_inc(split_lo, 1)
                body(0)
                repeat(dve, 10, lambda i: body(i + 1))

            def gated_down(name, gain, norm, split_at):
                for q in range(24):
                    g, c, m = q // 6, q // 2 % 3, q % 2
                    t = 2 * g + m
                    tile = T0[name] + t
                    if c == 2:
                        sum_tile(tile, tile % 4)
                        add_residual(t, tile, norm)
                    next_weights(4 * B0[name] + q)
                    if name == "dn0":
                        decay_constant(q)
                    if c == 2:
                        norm_lo(t, gain, split_at)

            residual_part("o", "ffn0", NORM["ffn0"], SPLIT["ffn0"])
            gated_up("up0", NORM["ffn0"], 0)
            gated_down("dn0", "mix1", NORM["mix1"], SPLIT["mix1"])

            for t in range(12):
                tile = T0["qkv"] + t
                if t == 0:
                    rms(NORM["mix1"])
                sum_tile(tile, t % 4)
                scale_tile(tile, t % 4, qkv[:, t, :])
                next_weights(4 * B0["qkv"] + t)
                if t in (6, 7):
                    j = t - 6
                    dve.wait_ge(head_std, j + 1)
                    dve.reciprocal(kinv[:, j, :], kstd[:, j, :]).then_inc(head_inv, 1)
                    dve.wait_ge(head_inv, j + 1)
                    dve.wait_ge(kgain_ready, 1)
                    dve.scalar_tensor_tensor(out=qkv[:, j, :], in0=qkv[:, j, :], scalar=kgain[:], in1=kinv[:, j, :],
                                             op0=ALU.mult, op1=ALU.mult).then_inc(k_ready, 1)
            dve.wait_ge(head_std, 3)
            dve.reciprocal(rq[:], qstd[:]).then_inc(head_inv, 1)
            dve.wait_ge(head_inv, 3)
            dve.wait_ge(bias_in, 16)
            dve.wait_ge(nsinks_ready, 1)

            def mask1(i):
                s = i % 2
                dve.wait_ge(scores, i + 1)
                if i >= 2:
                    dve.wait_ge(exped, i - 1)
                for b in range(2):
                    cols = slice(0, P) if b == 0 else slice(P, 3 * P)
                    for h in range(2):
                        j = 4 * i + 2 * b + h
                        ins = dve.scalar_tensor_tensor(out=sc1[:, s, h, cols], in0=bank[2 * s + h][:, cols],
                                                       scalar=rq[:, j:j + 1], in1=bias[:, 2 * i + h, cols],
                                                       op0=ALU.mult, op1=ALU.add)
                ins.then_inc(masked, 1)
                if i >= 1:
                    denominators(i - 1)
                dve.wait_ge(masked, i + 1)
                dve.tensor_reduce(mx[:, s, 0:2], sc1[:, s, :, 0:P], AX.X, ALU.max)
                dve.tensor_reduce(mx[:, s, 2:4], sc1[:, s, :, P:3 * P], AX.X, ALU.max).then_inc(maxed, 1)
                dve.wait_ge(maxed, i + 1)
                dve.scalar_tensor_tensor(out=nmx[:, s, :], in0=mx[:, s, :], scalar=-1.0,
                                         in1=nsinks[:, 4 * i:4 * i + 4], op0=ALU.mult, op1=ALU.min)\
                   .then_inc(nmx_ready, 1)
                dve.wait_ge(nmx_ready, i + 1)
                dve.tensor_tensor(mx[:, s, :], nmx[:, s, :], sinks[:, 4 * i:4 * i + 4], ALU.add).then_inc(negmax, 1)

            def denominators(i):
                s = i % 2
                dve.wait_ge(exped, i + 1)
                dve.tensor_tensor(den[:, s, :], den[:, s, :], esink[:, s, :], ALU.add).then_inc(den_step, 1)
                dve.wait_ge(den_step, 2 * i + 1)
                dve.reciprocal(rden[:, s, :], den[:, s, :]).then_inc(den_step, 1)

            for s in range(PAIRS1 + 3):
                if s < PAIRS1:
                    mask1(s)
                if s == PAIRS1:
                    denominators(s - 1)
                if s >= 3:
                    i = s - 3
                    dve.wait_ge(att_hi, i + 1)
                    dve.tensor_tensor(xb[:, i, 1, :], bank[STAT if i % 2 == 0 else OUT][:, 0:TOK],
                                      xb[:, i, 0, :].bitcast(F32), ALU.subtract).then_inc(att_lo, 1)

            residual_part("wo", "ffn1", NORM["ffn1"], SPLIT["ffn1"])
            gated_up("up1", NORM["ffn1"], 1)
            gated_down("dn1", "pre2", NORM["pre2"], SPLIT["pre2"])

            dve.memset(xl[:, :, 0:3], 0.0).then_inc(pad2_ready, 1)

            def mask2(i):
                s, h = i % 2, PAIRS1 + i
                dve.wait_ge(scores, h + 1)
                if i >= 2:
                    dve.wait_ge(exped, h - 1)
                dve.scalar_tensor_tensor(out=sc2[:, s, :], in0=bank[ATT + s][:, 0:3 * P], scalar=HD2 ** -0.5,
                                         in1=con("mask", 3 * P), op0=ALU.mult, op1=ALU.add).then_inc(masked, 1)
                dve.wait_ge(masked, h + 1)
                dve.tensor_reduce(mx[:, s, 0:1], sc2[:, s, 0:P], AX.X, ALU.max)
                dve.tensor_reduce(mx[:, s, 1:2], sc2[:, s, P:3 * P], AX.X, ALU.max).then_inc(maxed, 1)
                dve.wait_ge(maxed, h + 1)
                dve.tensor_scalar(nmx[:, s, :], mx[:, s, :], -1.0, None, ALU.mult).then_inc(negmax, 1)

            def normalise2(i):
                s, h = i % 2, PAIRS1 + i
                dve.wait_ge(exped, h + 1)
                dve.reciprocal(rden[:, s, :], den[:, s, :]).then_inc(den_step, 1)
                dve.wait_ge(den_step, 2 * PAIRS1 + i + 1)
                dve.tensor_scalar(pr2[:, s, 0:P], pr2[:, s, 0:P], rden[:, s, 0:1], None, ALU.mult)
                dve.tensor_scalar(pr2[:, s, P:3 * P], pr2[:, s, P:3 * P], rden[:, s, 1:2], None, ALU.mult)\
                   .then_inc(probs, 1)

            def xc_split(t):
                dve.wait_ge(xc_hi, t + 1)
                dve.tensor_tensor(xb[:, t, 1, :], xc[:, t, :], xb[:, t, 0, :].bitcast(F32), ALU.subtract)\
                   .then_inc(xc_lo, 1)

            def beside(r):
                if 0 <= r - CONV_AT < 17:
                    t, odd = divmod(r - CONV_AT, 2)
                    if not odd and t >= 1:
                        xc_split(t - 1)
                    for j in ((2, 3) if odd else (1,)):
                        if t == KT:
                            break
                        if j == 1:
                            dve.wait_ge(tap0, t + 1)
                        else:
                            dve.wait_ge(taps, 3 * t + j - 1)
                        dve.scalar_tensor_tensor(out=xc[:, t, :], in0=xl[:, t, j:j + TOK],
                                                 scalar=vec("conv2", 8 * j + t), in1=xc[:, t, :],
                                                 op0=ALU.mult, op1=ALU.add).then_inc(taps, 1)
                if 0 <= r - AT["v2"] - 2 < 16 and (r - AT["v2"]) % 2 == 0:
                    t = (r - AT["v2"] - 2) // 2
                    dve.wait_ge(a2_ready, t + 1)
                    dve.scalar_tensor_tensor(out=xl[:, t, 0:TOK], in0=sq[:, t % 2, :], scalar=1.0,
                                             in1=gate[:, t % 2, :], op0=ALU.add, op1=ALU.mult).then_inc(m_step, 1)
                if 0 <= r - AT["v2"] - 20 < 8:
                    t = r - AT["v2"] - 20
                    dve.wait_ge(bx_ready, t + 1)
                    dve.wait_ge(a_ready, t + 1)
                    dve.tensor_tensor_scan(xc[:, t, :], rr[:, t, :], xl[:, t, 0:TOK], 0.0, ALU.mult, ALU.add)\
                       .then_inc(scanned, 1)
                if head_of(r) is not None:
                    mask2(head_of(r))
                if head_of(r - 2) is not None:
                    normalise2(head_of(r - 2))
                if head_of(r - 5) is not None:
                    i = head_of(r - 5)
                    dve.wait_ge(att_hi, PAIRS1 + i + 1)
                    dve.tensor_tensor(xb[:, i, 1, :], bank[OUT][:, 0:TOK], xb[:, i, 0, :].bitcast(F32),
                                      ALU.subtract).then_inc(att_lo, 1)

            for r in range(AT["ba"]):
                n = R0 + r
                name = segment_of(r)
                if name == "rg":
                    part = r - AT["rg"]
                    if part == 0:
                        dve.wait_ge(scaled, SCALED["k2"] + 8)
                    for m in range(4):
                        if part == 1 or part == 2:
                            dve.wait_ge(r_ready, 4 * (part - 1) + m + 1)
                        if part == 3:
                            dve.wait_ge(i_ready, m + 1)
                        sum_tile(T0["rg"] + 4 * part + m, m)
                    next_weights(n)
                else:
                    t = r - AT[name]
                    tile = T0[name] + t
                    if name == "v2" and t < 4:
                        dve.wait_ge(i_ready, 4 + t + 1)
                    if name in POOL_SCALED:
                        if name == "v2":
                            if t >= 2:
                                dve.wait_ge(v2_turned, t - 1)
                            dst = vfm[:, t % 2, :]
                        else:
                            dst = DST[name][:, t, :]
                        sum_tile(tile, r % 4, dst)
                    else:
                        if r == 0:
                            rms(NORM["pre2"])
                        sum_tile(tile, r % 4)
                        scale_tile(tile, r % 4, xl[:, t, 3:TOK + 3] if name == "x2" else DST[name][:, t, :])
                    next_weights(n)
                beside(r)

            for t in range(8):
                tile = T0["ba"] + t
                sum_tile(tile, t % 4)
                dve.wait_ge(summed, tile + 1)
                dve.wait_ge(gates_ready, 1)
                dve.tensor_tensor(ga[:, t, :], ga[:, t, :], z[:, t % 4, :], ALU.mult).then_inc(gated_att, 1)
                next_weights(4 * B0["ba"] + t)
                for k in range(t - 1, t if t < 7 else 8):
                    if k >= 0:
                        dve.wait_ge(lru_hi, k + 1)
                        dve.tensor_tensor(xa[:, k, 1, :], xc[:, k, :], xa[:, k, 0, :].bitcast(F32), ALU.subtract)\
                           .then_inc(lru_lo, 1)

            def merged_lo(t):
                dve.wait_ge(mrg_hi, t + 1)
                dve.tensor_tensor(xb[:, t, 1, :], z[:, t % 4, :], xb[:, t, 0, :].bitcast(F32), ALU.subtract)\
                   .then_inc(mrg_lo, 1)

            dve.wait_ge(gates_ready, 2)
            for t in range(8):
                tile = T0["bl"] + t
                sum_tile(tile, t % 4)
                dve.wait_ge(summed, tile + 1)
                dve.tensor_tensor(z[:, t % 4, :], z[:, t % 4, :], gl[:, t, :], ALU.mult).then_inc(merge_step, 1)
                dve.wait_ge(merge_step, 2 * t + 1)
                dve.wait_ge(gated_att, t + 1)
                dve.tensor_tensor(z[:, t % 4, :], z[:, t % 4, :], ga[:, t, :], ALU.add).then_inc(merge_step, 1)
                next_weights(4 * B0["bl"] + t)
                dve.wait_ge(merge_step, 2 * t + 2)
                merged_lo(t)

            for t in range(8):
                sum_tile(T0["out2"] + t, t % 4, mix[:, t, :])
                next_weights(4 * B0["out2"] + t)

            def post_norm(src, gain, norm, t, at):
                if t >= 1:
                    dve.wait_ge(post_step, at + t)
                dve.scalar_tensor_tensor(out=z[:, t % 4, :], in0=src[:, t, :], scalar=vec(gain, t), in1=rbc[:],
                                         op0=ALU.mult, op1=ALU.mult).then_inc(post_step, 1)
                dve.wait_ge(post_step, at + t + 1)
                return dve.tensor_tensor(x[:, t, :], x[:, t, :], z[:, t % 4, :], ALU.add)

            rms(NORM["post2"])
            for t in range(8):
                post_norm(mix, "post2", NORM["post2"], t, 0).then_inc(resid, 1)
                if t >= 1:
                    norm_lo(t - 1, "mpre", SPLIT["mpre"])
            dve.wait_ge(resid, RESID[6] + 8)
            norm_lo(7, "mpre", SPLIT["mpre"])

            def up_lo(tile, slot):
                dve.wait_ge(split_hi, SPLIT["hid2"] + tile + 1)
                dve.tensor_tensor(hid[:, tile, 1, :], z[:, slot, :], hid[:, tile, 0, :].bitcast(F32),
                                  ALU.subtract).then_inc(split_lo, 1)

            def squared_up(i):
                for p in range(4):
                    tile = T0["mup"] + 4 * i + p
                    if isinstance(i, int) and i == 0 and p == 0:
                        rms(NORM["mpre"])
                        dve.tensor_tensor(rbc2[:], rbc[:], rbc[:], ALU.mult).then_inc(rbc2_ready, 1)
                    sum_tile(tile, p)
                    dve.wait_ge(summed, tile + 1)
                    dve.scalar_tensor_tensor(out=z[:, p, :], in0=z[:, p, :], scalar=0.0, in1=z[:, p, :],
                                             op0=ALU.max, op1=ALU.mult).then_inc(relu_ready, 1)
                    rest_weights(B0["mup"] + i + 1, p)
                    if p > 0 or not isinstance(i, int):
                        up_lo(4 * i + p - 1, (p - 1) % 4)
            squared_up(0)
            repeat(dve, 7, lambda i: squared_up(i + 1))
            up_lo(31, 3)
            for q in range(32):
                t = 2 * (q // 8) + q % 2
                if q // 2 % 4 == 3:
                    sum_tile(T0["mdn"] + t, (T0["mdn"] + t) % 4, mres[:, t, :])
                next_weights(4 * B0["mdn"] + q)
            rms(NORM["mpost"])
            for t in range(8):
                post_norm(mres, "mpost", NORM["mpost"], t, 8).then_inc(final, 1)

        @block.gpsimd
        def _(pool):
            def add_squares(norm):
                for t in range(1, 8):
                    pool.wait_ge(squared, 8 * norm + t + 1)
                    if t == 1:
                        if norm > 0:
                            pool.wait_ge(stat_ready, norm)
                        pool.tensor_tensor(ssum[:], sq[:, 0, :], sq[:, 1, :], ALU.add).then_inc(sq_added, 1)
                    else:
                        pool.wait_ge(sq_added, 7 * norm + t - 1)
                        pool.tensor_tensor(ssum[:], ssum[:], sq[:, t % 2, :], ALU.add).then_inc(sq_added, 1)

            def gates(name, norm, layer):
                base = 22 * layer
                pool.wait_ge(rbc_ready, norm + 1)

                def body(i):
                    for m in range(2):
                        pool.wait_ge(silu_ready, base + 2 * i + m + 1)
                        if not isinstance(i, int) or base:
                            pool.wait_ge(hval_ready, base + 2 * i)
                        pool.tensor_tensor(gate[:, m, :], act1[:, m, :], rbc[:], ALU.mult).then_inc(gate_ready, 1)
                body(0)
                repeat(pool, 10, lambda i: body(i + 1))

            add_squares(0)
            pool.wait_ge(pad_ready, 1)

            def products(i):
                for m in range(2):
                    pool.wait_ge(scaled, 4 * i + 3 + m)
                    pool.tensor_tensor(u[:, 2 * i + m, 2:TOK + 2], z[:, m, :], z[:, 2 + m, :], ALU.mult)\
                        .then_inc(u_ready, 1)

            def scaled_conv(t0):
                for t in (t0, t0 + 1):
                    pool.wait_ge(conv_step, 2 * t0 + 3 + t - t0)
                    pool.tensor_tensor(cv[:, t, :], cv[:, t, :], rbc[:], ALU.mult).then_inc(cv_ready, 1)
            for i in range(4):
                products(i)
                if i >= 2:
                    scaled_conv(2 * i - 4)
            scaled_conv(4)
            scaled_conv(6)
            add_squares(NORM["ffn0"])
            gates("up0", NORM["ffn0"], 0)
            add_squares(NORM["mix1"])
            for i in range(PAIRS1):
                s = i % 2
                pool.wait_ge(exped, i + 1)
                pool.wait_ge(den_step, 2 * i + 2)
                for b in range(2):
                    cols, n = (slice(0, P), P) if b == 0 else (slice(P, 3 * P), 2 * P)
                    ins = pool.tensor_tensor(pr1[:, s, :, cols], pr1[:, s, :, cols],
                                             rden[:, s, 2 * b:2 * b + 2].unsqueeze(2).to_broadcast([P, 2, n]),
                                             ALU.mult)
                ins.then_inc(normed, 1)
            add_squares(NORM["ffn1"])
            gates("up1", NORM["ffn1"], 1)
            add_squares(NORM["pre2"])

            def rope(j):
                src, t = (q2, j) if j < 8 else (k2, j - 8)
                rows = src[0:ROT, t, :]
                pool.wait_ge(scaled, SCALED["q2" if j < 8 else "k2"] + t + 1)
                if j >= 2:
                    pool.wait_ge(roped, j - 1)
                pool.tensor_tensor(rtmp[:, j % 2, 0, :], rows, con("cos", TOK, ROT), ALU.mult).then_inc(rot_cos, 1)
                pool.wait_ge(rot_out, j + 1)
                pool.tensor_tensor(rtmp[:, j % 2, 1, :], rtmp[:, j % 2, 1, :], con("sin", TOK, ROT), ALU.mult)\
                    .then_inc(rot_prod, 1)
                pool.wait_ge(rot_cos, j + 1)
                pool.wait_ge(rot_prod, j + 1)
                pool.tensor_tensor(rows, rtmp[:, j % 2, 0, :], rtmp[:, j % 2, 1, :], ALU.add).then_inc(roped, 1)

            def scale(name, t):
                dst = vfm[:, t % 2, :] if name == "v2" else DST[name][:, t, :]
                pool.wait_ge(summed, T0[name] + t + 1)
                pool.tensor_tensor(dst, dst, rbc[:], ALU.mult).then_inc(pool_scaled, 1)

            for j in range(16):
                rope(j)
            pool.wait_ge(xc_lo, KT)
            for t in range(KT):
                pool.wait_ge(i_ready, t + 1)
                pool.tensor_tensor(xc[:, t, :], xc[:, t, :], act1[:, t % 2, :], ALU.mult).then_inc(ix_ready, 1)
            for t in range(KT):
                scale("v2", t)
            for t in range(KT):
                scale("g2", t)
            for t in range(KT):
                scale("ga", t)
                if 2 <= t < 6:
                    if t == 2:
                        pool.wait_ge(mult_ready, 1)
                    for k in (2 * t - 4, 2 * t - 3):
                        pool.wait_ge(ix_ready, k + 1)
                        pool.tensor_tensor(xl[:, k, 0:TOK], xl[:, k, 0:TOK], xc[:, k, :], ALU.mult)\
                            .then_inc(bx_ready, 1)
            pool.wait_ge(gelu_ready, 1)
            for t in range(KT):
                scale("gl", t)
                for k in ((2 * t - 8, 2 * t - 7) if t >= 4 else ()):
                    pool.wait_ge(scanned, k + 1)
                    pool.tensor_tensor(xc[:, k, :], xc[:, k, :], g2[:, k, :], ALU.mult).then_inc(lru_ready, 1)
            add_squares(NORM["post2"])
            add_squares(NORM["mpre"])
            pool.wait_ge(rbc2_ready, 1)

            def square_relu(i):
                for p in range(4):
                    pool.wait_ge(relu_ready, 4 * i + p + 1)
                    pool.tensor_tensor(z[:, p, :], z[:, p, :], rbc2[:], ALU.mult).then_inc(sqrelu_ready, 1)
            repeat(pool, 8, square_relu)
            add_squares(NORM["mpost"])


def _tiles(v):
    return np.asarray(v).reshape(-1, P).T


def _chunk(w, rows, cols):
    part = w[rows][:, cols]
    return part.reshape(-1, P, 2, P).transpose(1, 2, 0, 3).reshape(-1)


def _stream(w):
    out = []

    def columns(m, cols, rows=slice(0, D)):
        out.append(_chunk(m, rows, cols))

    def cols(start):
        return np.arange(start, start + 2 * P)

    def gated(layer):
        gu, dn = w["ffn_w_gate_up"][layer], w["ffn_w_down"][layer]
        for j in range(FF // 256):
            columns(gu, cols(256 * j))
            columns(gu, cols(FF + 256 * j))
        for g in range(4):
            for k0, kts in GROUP_K:
                columns(dn, cols(256 * g), slice(k0 * P, (k0 + kts) * P))

    w_in = w["conv_w_in"][0]
    for j in range(4):
        columns(w_in, cols(256 * j))
        columns(w_in, cols(2 * D + 256 * j))
    for j in range(4):
        columns(w_in, cols(D + 256 * j))
    for j in range(4):
        columns(w["conv_w_out"][0], cols(256 * j))
    gated(0)
    order = np.concatenate([np.arange(HD1 * head1(i), HD1 * head1(i) + HD1) for i in range(HEADS1)])
    qkv = w["attn_w_qkv"][0]
    order_all = np.concatenate([np.arange(D, D + 2 * KV1 * HD1), order])
    for j in range(6):
        columns(qkv, order_all[256 * j:256 * j + 256])
    wo = w["attn_w_o"][0][order]
    for j in range(4):
        columns(wo, cols(256 * j))
    gated(1)
    w_in = w["w_in_2"][0]
    part = {"q2": 0, "k2": 1, "v2": 2, "x2": 3, "g2": 4, "ga": 5, "gl": 6}
    for name in ("x2", "q2", "k2", "rg", "v2", "g2", "ga", "gl"):
        if name == "rg":
            for m in (w["w_rg_a_2"][0], w["w_rg_i_2"][0]):
                six = m.reshape(2, 2, 2, P, 2, P)
                out.append(six.transpose(3, 0, 1, 4, 2, 5).reshape(-1))
        else:
            for j in range(4):
                columns(w_in, cols(D * part[name] + 256 * j))
    for name in ("w_branch_attn_2", "w_branch_lru_2", "w_out_2"):
        for j in range(4):
            columns(w[name][0], cols(256 * j))
    for j in range(FF2 // 256):
        columns(w["w_mlp_up_2"][0], cols(256 * j))
    for g in range(4):
        for c in range(4):
            columns(w["w_mlp_down_2"][0], cols(256 * g), slice(c * D, (c + 1) * D))
    return np.concatenate(out)


def _constants():
    c = np.zeros((P, NCON), np.float32)
    c[:, 0:P] = 1.0
    c[0:64, 128:192] = 1.0
    c[64:128, 192:256] = 1.0
    c[:, 256:384] = np.eye(P, dtype=np.float32)
    q, k = np.arange(P)[:, None], np.arange(P)[None, :]
    c[:, 384:768] = np.concatenate([np.where(q >= k, 0, -BIG), np.zeros((P, P)), np.where(q >= k, 0, -BIG)], 1)
    half = ROT // 2
    freq = np.float32(500000.0) ** (-np.arange(0, ROT, 2, dtype=np.float32) / np.float32(ROT))
    angle = np.arange(TOK, dtype=np.float32)[:, None] * freq.astype(np.float32)[None, :]
    c[0:ROT, 768:1024] = np.tile(np.cos(angle).T, (2, 1))
    c[0:ROT, 1024:1280] = np.tile(np.sin(angle).T, (2, 1))
    for j in range(half):
        c[half + j, 1280 + j] = -1.0
        c[j, 1280 + half + j] = 1.0
    return c


def _bias():
    q, k = np.arange(P)[:, None], np.arange(P)[None, :]
    own = np.where(q >= k, q - k, BIG)
    before = np.where(k > q, q + P - k, BIG)
    dist = np.concatenate([own, before, own], 1).astype(np.float32)
    slopes = [np.float32(2.0) ** np.float32(-8.0 * (head1(i) + 1) / HEADS1) for i in range(HEADS1)]
    return np.concatenate([-s * dist for s in slopes], 1)


_NAMES = ["bias", "x", "stream", "vecs", "sinks", "cons"]


def kernel(**inputs):
    import concourse.bacc as _bacc
    from concourse.bass_utils import run_bass_kernel_spmd as _run

    w = {k: np.asarray(v) for k, v in inputs.items()}
    f = _tiles
    vecs = [f(w["norm_mixer"][0]), f(w["norm_ffn"][0]), f(w["norm_mixer"][1]), f(w["norm_ffn"][1]),
            f(w["conv_w"][0][0]), f(w["conv_w"][0][1]), f(w["conv_w"][0][2]),
            f(np.concatenate([w["attn_q_gain"][0]] * 2)), f(np.concatenate([w["attn_k_gain"][0]] * 2)),
            f(w["attn_pre_norm_2"][0]), f(w["attn_post_norm_2"][0]),
            *[f(w["conv_w_2"][0][j]) for j in range(4)], f(w["conv_b_2"][0]),
            f(w["b_rg_a_2"][0]), f(w["b_rg_i_2"][0]), f(w["lru_lambda_2"][0]),
            f(w["mlp_pre_norm_2"][0]), f(w["mlp_post_norm_2"][0])]
    arrays = {
        "x": w["x"][0].T.reshape(KT, P, TOK).transpose(1, 0, 2),
        "stream": _stream(w),
        "vecs": np.concatenate(vecs, 1),
        "sinks": np.broadcast_to(w["attn_sinks"][0][[head1(2 * t + h) for t in range(PAIRS1) for _ in range(2)
                                                     for h in range(2)]][None, :], (P, 4 * PAIRS1)),
        "bias": _bias(),
        "cons": _constants(),
    }
    nc = _bacc.Bacc("TRN2", target_bir_lowering=False, num_devices=1, dynamic_dma_scratch_size=1024)
    held, args = {}, []
    for name in _NAMES:
        a = np.ascontiguousarray(arrays[name])
        held[f"in_{name}"] = a
        args.append(nc.dram_tensor(f"in_{name}", a.shape, mybir.dt.from_np(a.dtype), kind="ExternalInput").ap())
    args.append(nc.dram_tensor("out_0", (P, KT, TOK), F32, kind="ExternalOutput").ap())
    build(nc, *args)
    r = _run(nc, [held], core_ids=[0])
    got = r.results[0]["out_0"]
    return np.ascontiguousarray(got.transpose(1, 0, 2).reshape(D, TOK).T)[None]
```

```python
from contextlib import ExitStack

import concourse.bass as bass
from concourse import mybir
import numpy as np

F32 = mybir.dt.float32
F32R = mybir.dt.float32r
ACT = mybir.ActivationFunctionType
ALU = mybir.AluOpType
AX = mybir.AxisListType

P = 128
TOK = 256
D = 1024
KT = D // P
WARMING = 9
EPS = 1e-6
FF = 2816
FT = FF // P
HEADS1, KV1, HD1 = 16, 4, 64
HEADS2, HD2 = 8, 128
FF2 = 4096
ROT = 32
ROWS = 48
PIECE = 8 * P
BIG = 1e30

BODIES = [("bx", 4), ("c", 2), ("o", 2), ("up0", 11), ("dn0", 6),
          ("qkv", 3), ("wo", 2), ("up1", 11), ("dn1", 6),
          ("x2", 2), ("q2", 2), ("k2", 2), ("rg", 1), ("v2", 2), ("g2", 2), ("ga", 2), ("gl", 2),
          ("ba", 2), ("bl", 2), ("out2", 2), ("mup", 8), ("mdn", 8)]
TILES = {"bx": 16, "c": 8, "o": 8, "up0": 44, "dn0": 8, "qkv": 12, "wo": 8, "up1": 44, "dn1": 8,
         "x2": 8, "q2": 8, "k2": 8, "rg": 16, "v2": 8, "g2": 8, "ga": 8, "gl": 8,
         "ba": 8, "bl": 8, "out2": 8, "mup": 32, "mdn": 8}
B0, T0 = {}, {}
_b = _t = 0
for _name, _n in BODIES:
    B0[_name], T0[_name] = _b, _t
    _b += _n
    _t += TILES[_name]
ALL_BODIES = _b
GROUP_K = [(0, 8), (8, 8), (16, 6)]


def blocks_of(n):
    for name in ("dn0", "dn1"):
        first = 4 * B0[name]
        if first <= n < first + 24:
            return GROUP_K[(n - first) // 2 % 3][1]
    return 8


def chunk_offset(c):
    short = 0
    for name in ("dn0", "dn1"):
        first = 2 * B0[name]
        short += sum(1 for j in range(4) if first + 3 * j + 2 < c)
    return c * 2 * P * PIECE - short * 2 * P * 2 * P


def vec_columns():
    at, out = 0, {}
    for name, n in [("mix0", 8), ("ffn0", 8), ("mix1", 8), ("ffn1", 8), ("conv", 24), ("qg", 1), ("kg", 1),
                    ("pre2", 8), ("post2", 8), ("conv2", 32), ("convb2", 8), ("ba", 8), ("bi", 8),
                    ("lam", 8), ("mpre", 8), ("mpost", 8)]:
        out[name] = at
        at += n
    return out, at


VEC, NVEC = vec_columns()
CON = {"ones": 0, "half": 128, "ident": 256, "mask": 384, "cos": 768, "sin": 1024}
NCON = 1280
PAIRS1 = HEADS1 // 2


def head1(i):
    tile, half = divmod(i, 2)
    return 4 * (2 * (tile // 4) + half) + tile % 4


def build(nc, bias_in_dram, x_in, stream, vecs_in, sinks_in, cons_in, out):
    with ExitStack() as ctx:
        sb = lambda n, s, d=F32: ctx.enter_context(nc.sbuf_tensor(n, s, d))
        sem = lambda n: ctx.enter_context(nc.semaphore(n))

        raw = sb("raw", [P, 4, 2 * PIECE])
        whi = sb("whi", [P, 4, 8, P], F32R)
        wlo = sb("wlo", [P, 4, 8, P], F32R)
        x = sb("x", [P, KT, TOK])
        xa = sb("xa", [P, KT, 2, TOK], F32R)
        xb = sb("xb", [P, KT, 2, TOK], F32R)
        spill = sb("spill", [P, 4, TOK])
        z = sb("z", [P, 4, TOK])
        act1 = sb("act1", [P, 2, TOK])
        gate = sb("gate", [P, 2, TOK])
        sq = sb("sq", [P, 2, TOK])
        ssum = sb("ssum", [P, TOK])
        rstd = sb("rstd", [P, TOK])
        rinv = sb("rinv", [P, 2])
        rbc = sb("rbc", [P, TOK])
        vecs = sb("vecs", [P, NVEC])
        cons = sb("cons", [P, NCON])
        sinks = sb("sinks", [P, 4 * PAIRS1])
        nsinks = sb("nsinks", [P, 4 * PAIRS1])
        kgain = sb("kgain", [P, 1])
        lamb = sb("lamb", [P, 6, KT])
        lam8 = sb("lam8", [P, KT])
        nlam8 = sb("nlam8", [P, KT])
        rtmp = sb("rtmp", [ROWS, 2, 2, TOK])
        rbc2 = sb("rbc2", [P, TOK])
        scratch = sb("scratch", [P, 1])
        mx = sb("mx", [P, 2, 4])
        nmx = sb("nmx", [P, 2, 4])
        den = sb("den", [P, 2, 4])
        esink = sb("esink", [P, 2, 4])
        rden = sb("rden", [P, 2, 4])

        region = ExitStack()
        hid = region.enter_context(nc.sbuf_tensor("hid", [P, 32, 2, TOK], F32R))
        mres = region.enter_context(nc.sbuf_tensor("mres", [P, KT, TOK], F32))
        region.close()
        region0 = ExitStack()
        u = region0.enter_context(nc.sbuf_tensor("u", [P, KT, TOK + 2], F32))
        cv = region0.enter_context(nc.sbuf_tensor("cv", [P, KT, TOK], F32))
        region0.close()
        region1 = ExitStack()
        sb1 = lambda n, s: region1.enter_context(nc.sbuf_tensor(n, s, F32))
        qkv = sb1("qkv", [P, 12, TOK])
        kstd = sb1("kstd", [P, 2, TOK])
        kinv = sb1("kinv", [P, 2, TOK])
        vtok = sb1("vtok", [P, 2, TOK])
        sc1 = sb1("sc1", [P, 2, 2, 3 * P])
        pr1 = sb1("pr1", [P, 2, 2, 3 * P])
        pt1 = sb1("pt1", [P, 2, 3 * P])
        qstd = sb1("qstd", [P, 32])
        rq = sb1("rq", [P, 32])
        sb1("unused1", [P, 22 * 2 * TOK - (12 + 2 + 2 + 2) * TOK - 2 * 2 * 2 * 384 - 2 * 384 - 64])
        bias = sb1("bias", [P, HEADS1, 3 * P])
        region1.close()
        region2 = ExitStack()
        sb2 = lambda n, s: region2.enter_context(nc.sbuf_tensor(n, s, F32))
        q2 = sb2("q2", [P, HEADS2, TOK])
        k2 = sb2("k2", [P, HEADS2, TOK])
        vfm = sb2("vfm", [P, 2, TOK])
        vtok2 = sb2("vtok2", [P, 2, D])
        xl = sb2("xl", [P, KT, TOK + 3])
        xc = sb2("xc", [P, KT, TOK])
        rr = sb2("rr", [P, KT, TOK])
        g2 = sb2("g2", [P, KT, TOK])
        ga = sb2("ga", [P, KT, TOK])
        gl = sb2("gl", [P, KT, TOK])
        sc2 = sb2("sc2", [P, 2, 3 * P])
        pr2 = sb2("pr2", [P, 2, 3 * P])
        pt2 = sb2("pt2", [P, 2, 3 * P])
        region2.close()
        mix = q2

        bank = [ctx.enter_context(nc.psum_tensor(f"bank{i}", [P, 512], F32)) for i in range(8)]
        SUMS = 508
        STAT, ATT, OUT = 4, 5, 7

        con = lambda name, n, rows=P: cons[0:rows, CON[name]:CON[name] + n]
        vec = lambda name, i: vecs[:, VEC[name] + i:VEC[name] + i + 1]

        small_in = sem("small_in")
        vecs_loaded = sem("vecs_loaded")
        x_loaded = [sem("x_loaded0"), sem("x_loaded1")]
        first_raw = [sem("first_raw0"), sem("first_raw1")]
        raw_loaded = [sem("raw_loaded0"), sem("raw_loaded1")]
        hi_ready = sem("hi_ready")
        lo_ready = sem("lo_ready")
        piece_done = sem("piece_done")
        spilled = sem("spilled")
        summed = sem("summed")
        scaled = sem("scaled")
        split_hi = sem("split_hi")
        split_lo = sem("split_lo")
        resid = sem("resid")
        squared = sem("squared")
        sq_added = sem("sq_added")
        stat_ready = sem("stat_ready")
        rstd_ready = sem("rstd_ready")
        rinv_ready = sem("rinv_ready")
        spread_ready = sem("spread_ready")
        rbc_ready = sem("rbc_ready")
        pad_ready = sem("pad_ready")
        warm_ready = sem("warm_ready")
        u_ready = sem("u_ready")
        tap_ready = sem("tap_ready")
        conv_step = sem("conv_step")
        cv_ready = sem("cv_ready")
        cy_ready = sem("cy_ready")
        silu_ready = sem("silu_ready")
        gate_ready = sem("gate_ready")
        hval_ready = sem("hval_ready")
        kgain_ready = sem("kgain_ready")
        nsinks_ready = sem("nsinks_ready")
        bias_in = sem("bias_in")
        head_sq = sem("head_sq")
        head_stat = sem("head_stat")
        head_std = sem("head_std")
        head_inv = sem("head_inv")
        k_ready = sem("k_ready")
        v_turned = sem("v_turned")
        v_ready = sem("v_ready")
        scores = sem("scores")
        masked = sem("masked")
        maxed = sem("maxed")
        nmx_ready = sem("nmx_ready")
        negmax = sem("negmax")
        exped = sem("exped")
        den_step = sem("den_step")
        normed = sem("normed")
        probs = sem("probs")
        pt_turned = sem("pt_turned")
        pt_ready = sem("pt_ready")
        att_out = sem("att_out")
        att_copied = sem("att_copied")
        att_hi = sem("att_hi")
        att_lo = sem("att_lo")
        pad2_ready = sem("pad2_ready")
        lam_step = sem("lam_step")
        lam_act = sem("lam_act")
        rot_cos = sem("rot_cos")
        rot_out = sem("rot_out")
        rot_prod = sem("rot_prod")
        pool_scaled = sem("pool_scaled")
        a2_ready = sem("a2_ready")
        roped = sem("roped")
        v2_turned = sem("v2_turned")
        v2_ready = sem("v2_ready")
        tap0 = sem("tap0")
        taps = sem("taps")
        xc_hi = sem("xc_hi")
        xc_lo = sem("xc_lo")
        r_ready = sem("r_ready")
        i_ready = sem("i_ready")
        ix_ready = sem("ix_ready")
        a_ready = sem("a_ready")
        m_step = sem("m_step")
        mult_ready = sem("mult_ready")
        bx_ready = sem("bx_ready")
        scanned = sem("scanned")
        gelu_ready = sem("gelu_ready")
        lru_ready = sem("lru_ready")
        lru_hi = sem("lru_hi")
        lru_lo = sem("lru_lo")
        gates_ready = sem("gates_ready")
        gated_att = sem("gated_att")
        gated_lru = sem("gated_lru")
        merged = sem("merged")
        mrg_hi = sem("mrg_hi")
        mrg_lo = sem("mrg_lo")
        post_step = sem("post_step")
        rbc2_ready = sem("rbc2_ready")
        relu_ready = sem("relu_ready")
        sqrelu_ready = sem("sqrelu_ready")
        gained = sem("gained")
        end_step = sem("end_step")
        final = sem("final")
        final_pool = sem("final_pool")
        stored = sem("stored")

        SPLIT = {"mix0": 0, "cy": 8, "ffn0": 16, "hid0": 24, "mix1": 46, "ffn1": 54, "hid1": 62, "pre2": 84,
                 "mpre": 92, "hid2": 100}
        SCALED = {"bx": 0, "up0": 16, "qkv": 38, "up1": 50, "x2": 72, "q2": 80, "k2": 88}
        POOL_SCALED = {"v2": 0, "g2": 8, "ga": 16, "gl": 24}
        NORM = {"mix0": 0, "ffn0": 1, "mix1": 2, "ffn1": 3, "pre2": 4, "post2": 5, "mpre": 6, "mpost": 7}
        TURNED = {NORM[name]: i for i, name in enumerate(("mix0", "post2", "mpre", "mpost"))}
        SQ0 = [sum(6 if m in TURNED else 7 for m in range(n)) for n in range(9)]
        RESID = {1: 0, 2: 8, 3: 16, 4: 24, 6: 32}
        R0 = 4 * B0["x2"]
        AT = {name: 4 * B0[name] - R0 for name in ("x2", "q2", "k2", "rg", "v2", "g2", "ga", "gl", "ba")}
        CONV_AT = AT["q2"] - 4
        HEAD_AT = AT["v2"] + 5
        DST = {"x2": xl, "q2": q2, "k2": k2, "g2": g2, "ga": ga, "gl": gl}

        def segment_of(r):
            return [name for name in AT if AT[name] <= r][-1]

        def head_of(r):
            i, odd = divmod(r - HEAD_AT, 3)
            return i if not odd and 0 <= i < HEADS2 else None

        def repeat(eng, count, body):
            if count >= 3:
                with eng.Fori(0, count) as i:
                    body(i)
            else:
                for i in range(count):
                    body(i)

        block = ctx.enter_context(nc.Block())

        @block.sync
        def _(sp):
            sp.dma_start(vecs[:], vecs_in).then_inc(vecs_loaded, 16)
            sp.dma_start(x[:, 0:4, :], x_in[:, 0:4, :]).then_inc(x_loaded[0], 16)
            for p in range(4):
                at = chunk_offset(p // 2)
                src = stream[at:at + 2 * P * PIECE].rearrange("(p n) -> p n", p=P)
                half = slice(p % 2 * PIECE, (p % 2 + 1) * PIECE)
                sp.dma_start(raw[:, p // 2, half], src[:, half])\
                  .then_inc(first_raw[p // 2] if p % 2 == 0 else raw_loaded[p // 2], 16)
                if p == 1:
                    sp.dma_start(x[:, 4:8, :], x_in[:, 4:8, :]).then_inc(x_loaded[1], 16)
            def load(b, h, offset, size, waits):
                if waits:
                    if h == 1:
                        sp.wait_ge(lo_ready, 4 * b - 4)
                    sp.wait_ge(raw_loaded[h], 16 * b)
                    if h == 0:
                        sp.wait_ge(lo_ready, 4 * b - 6)
                    sp.wait_ge(x_loaded[1], 16)
                src = stream[bass.ds(offset, P * size)].rearrange("(p n) -> p n", p=P)
                sp.dma_start(raw[:, (b % 2) * 2 + h, 0:size], src).then_inc(raw_loaded[h], 16)

            def loads(first, count):
                def body(i):
                    for h in range(2):
                        load(first + i, h, chunk_offset(2 * first) + (2 * i + h) * 2 * P * PIECE, 2 * PIECE, True)
                repeat(sp, count, body)

            sp.dma_start(cons[:], cons_in).then_inc(small_in, 16)
            sp.dma_start(sinks[:], sinks_in).then_inc(small_in, 16)
            for h in range(2):
                sp.wait_ge(raw_loaded[h], 16)
                load(1, h, chunk_offset(2 + h), 2 * PIECE, False)
            loads(2, 5)
            sp.dma_start(bias[:].rearrange("p h k -> p (h k)"), bias_in_dram).then_inc(bias_in, 16)
            loads(7, B0["dn0"] - 7)
            for name, after in (("dn0", "qkv"), ("dn1", "x2")):
                for c in range(12):
                    load(B0[name] + c // 2, c % 2, chunk_offset(2 * B0[name] + c), 2 * GROUP_K[c % 3][1] * P, True)
                if after == "qkv":
                    loads(B0["qkv"], B0["dn1"] - B0["qkv"])
            loads(B0["x2"], ALL_BODIES - B0["x2"])
            for t in (0, 1, 6, 2, 3, 7, 4, 5):
                if t < 6:
                    sp.wait_ge(final, t + 1)
                else:
                    sp.wait_ge(final_pool, t - 5)
                sp.dma_start(out[:, t, :], x[:, t, :]).then_inc(stored, 16)
            sp.wait_ge(stored, 16 * KT)

        @block.tensor
        def _(pe):
            def blocks(slot, X, tiles, dst, first, last, at=0):
                for i, k in enumerate(tiles):
                    pe.matmul(dst[:, :], whi[:, slot, at + i, :], X[:, k, :, :],
                              start=first and i == 0, stop=False)
                    ins = pe.matmul(dst[:, 0:TOK], wlo[:, slot, at + i, :], X[:, k, 0, :],
                                    start=False, stop=last and i == len(tiles) - 1)
                return ins

            def segment(name, X, split, extra=None):
                count = dict(BODIES)[name]

                def body(i):
                    for p in range(4):
                        n = 4 * (B0[name] + i) + p
                        tile = T0[name] + 4 * i + p
                        pe.wait_ge(lo_ready, n + 1)
                        if T0[name] >= 4:
                            pe.wait_ge(summed, tile - 3)
                        elif isinstance(i, int) and tile >= 4:
                            pe.wait_ge(summed, tile - 3)
                        blocks(p, X, range(8), bank[p], True, True).then_inc(piece_done, 1)
                        if extra:
                            extra(4 * i + p)
                split()
                if extra:
                    for i in range(count):
                        body(i)
                else:
                    repeat(pe, count, body)

            def stat(norm):
                if norm == 0:
                    pe.wait_ge(small_in, 32)
                pe.wait_ge(sq_added, SQ0[norm + 1])
                if norm not in TURNED:
                    pe.matmul(bank[STAT][:, 0:TOK], con("ones", P), ssum[:], start=True, stop=True)\
                      .then_inc(stat_ready, 1)
                    return
                for tb in range(2):
                    pe.matmul(bank[STAT][:, SUMS + tb:SUMS + tb + 1], ssum[:, tb * P:(tb + 1) * P], con("ones", 1),
                              start=True, stop=False)
                    if tb == 0:
                        pe.wait_ge(squared, 8 * norm + 8)
                    ins = pe.matmul(bank[STAT][:, SUMS + tb:SUMS + tb + 1], sq[:, 1, tb * P:(tb + 1) * P],
                                    con("ones", 1), start=False, stop=True)
                ins.then_inc(stat_ready, 1)

            def keep_warm(count):
                for _ in range(count):
                    pe.matmul(bank[ATT][:, 0:TOK], con("ones", P), cons[:, 0:TOK], start=True, stop=True)

            def spread(norm):
                pe.wait_ge(rinv_ready, TURNED[norm] + 1)
                for tb in range(2):
                    ins = pe.matmul(bank[STAT][:, tb * P:(tb + 1) * P], rinv[:, tb:tb + 1].to_broadcast([P, P]),
                                    con("ident", P), start=True, stop=True)
                ins.then_inc(spread_ready, 1)

            def first_body(name, X, norm, split, split_at, order):
                seen = 0
                for step in order:
                    if step == "norm":
                        if norm is not None:
                            stat(norm)
                        continue
                    if step == "spread":
                        if norm is not None:
                            spread(norm)
                        continue
                    a, b, p = step
                    n, tile = 4 * B0[name] + p, T0[name] + p
                    if a == 0:
                        pe.wait_ge(lo_ready, n + 1)
                        if tile >= 4:
                            pe.wait_ge(summed, tile - 3)
                    for k in range(a, b):
                        if k >= seen:
                            pe.wait_ge(split, split_at + k + 1)
                            seen = k + 1
                        ins = blocks(p, X, [k], bank[p], k == 0, k == KT - 1, at=k)
                    if b == KT:
                        ins.then_inc(piece_done, 1)

            STAIR = [(0, 6, 0), (0, 5, 1), (0, 4, 2), "norm", (0, 3, 3), (6, 8, 0), (5, 8, 1), (4, 8, 2), (3, 8, 3)]
            ONE_BY_ONE = [(k, k + 1, p) for k in range(KT - 3) for p in range(4)] \
                + [(KT - 3, KT, 0), (KT - 3, KT, 1), "norm", (KT - 3, KT, 2), "spread", (KT - 3, KT, 3)]
            AS_LOADED = [(0, 4, 0), (0, 4, 1), (4, 8, 0), (4, 8, 1), (0, 8, 2), "norm", (0, 4, 3), "spread", (4, 8, 3)]
            IN_ORDER = [(0, 8, p) for p in range(4)]

            def rest(name, X, extra=None):
                count = dict(BODIES)[name] - 1

                def body(i):
                    for p in range(4):
                        pe.wait_ge(lo_ready, 4 * (B0[name] + 1 + i) + p + 1)
                        pe.wait_ge(summed, T0[name] + 4 * (1 + i) + p - 3)
                        blocks(p, X, range(8), bank[p], True, True).then_inc(piece_done, 1)
                        if extra:
                            extra(4 * (1 + i) + p)
                if extra:
                    for i in range(count):
                        body(i)
                else:
                    repeat(pe, count, body)

            def gated_down(name, split_at):
                for q in range(24):
                    g, c, m = q // 6, q // 2 % 3, q % 2
                    k0, kts = GROUP_K[c]
                    n, tile = 4 * B0[name] + q, T0[name] + 2 * g + m
                    pe.wait_ge(lo_ready, n + 1)
                    if q == 0:
                        pe.wait_ge(split_lo, split_at + 20)
                    if q == 4:
                        pe.wait_ge(split_lo, split_at + FT)
                    if c == 0:
                        pe.wait_ge(summed, tile - 3)
                    blocks(n % 4, hid, range(k0, k0 + kts), bank[tile % 4], c == 0, c == 2)\
                        .then_inc(piece_done, 1)

            pe.wait_ge(warm_ready, 1)
            for i in range(WARMING):
                pe.matmul(bank[ATT][:, 0:TOK], pt1[:, 0, 0:P], pt1[:, 1, 0:TOK], start=True, stop=True)
            first_body("bx", xa, NORM["mix0"], split_lo, SPLIT["mix0"], AS_LOADED)
            rest("bx", xa)
            def c_tiles():
                for i in range(8):
                    pe.wait_ge(lo_ready, 4 * B0["c"] + i + 1)
                    pe.wait_ge(summed, T0["c"] + i - 3)
                    blocks(i % 4, xa, range(8), bank[i % 4], True, True).then_inc(piece_done, 1)
            c_tiles()
            first_body("o", xb, None, split_lo, SPLIT["cy"], STAIR)
            rest("o", xb)
            first_body("up0", xa, NORM["ffn0"], split_lo, SPLIT["ffn0"], STAIR)
            rest("up0", xa)
            gated_down("dn0", SPLIT["hid0"])

            def head_sums(i):
                t = i - 1
                if 0 <= t < 2:
                    pe.wait_ge(head_sq, t + 1)
                    pe.matmul(bank[ATT + t][:, 0:TOK], con("half", P), sq[:, t, :],
                              start=True, stop=True).then_inc(head_stat, 1)
                if 4 <= t < 12:
                    pe.wait_ge(head_sq, t - 1)
                    for tb in range(2):
                        at = TOK + 4 * (t - 4) + 2 * tb
                        ins = pe.matmul(bank[STAT][:, at:at + 2], sq[:, t % 2, tb * P:(tb + 1) * P],
                                        con("half", P)[:, 0:P:P // 2], start=True, stop=True)
                    ins.then_inc(head_stat, 1)
            first_body("qkv", xa, NORM["mix1"], split_lo, SPLIT["mix1"], STAIR)
            for i in range(4, 12):
                pe.wait_ge(lo_ready, 4 * B0["qkv"] + i + 1)
                pe.wait_ge(summed, T0["qkv"] + i - 3)
                blocks(i % 4, xa, range(8), bank[i % 4], True, True).then_inc(piece_done, 1)
                if i < 6:
                    head_sums(i - 3)
                if i == 6:
                    pe.wait_ge(scaled, SCALED["qkv"] + 4)
                    for f in range(2):
                        for tb in range(2):
                            ins = pe.transpose(bank[OUT][:, (2 * tb + f) * P:(2 * tb + f + 1) * P],
                                               qkv[:, 2 + f, tb * P:(tb + 1) * P], con("ident", P))
                    ins.then_inc(v_turned, 1)
                head_sums(i if i >= 5 else 0)
            head_sums(12)

            def scores1(i):
                if i >= 2:
                    pe.wait_ge(masked, i - 1)
                for cols, q_cols, k_cols in ((slice(0, P), slice(0, P), slice(0, P)),
                                             (slice(P, 3 * P), slice(P, 2 * P), slice(0, 2 * P))):
                    for h in range(2):
                        rows = slice(64 * h, 64 * h + 64)
                        ins = pe.matmul(bank[2 * (i % 2) + h][:, cols], qkv[rows, 4 + i, q_cols],
                                        qkv[rows, i // 4, k_cols], start=True, stop=True)
                ins.then_inc(scores, 1)

            def turn1(i):
                pe.wait_ge(normed, i + 1)
                if i >= 1:
                    pe.wait_ge(pt_ready, i)
                for h in range(2):
                    for j in range(3):
                        ins = pe.transpose(bank[ATT + h][:, j * P:(j + 1) * P], pr1[:, i % 2, h, j * P:(j + 1) * P],
                                           con("ident", P))
                ins.then_inc(pt_turned, 1)

            def values1(i):
                pe.wait_ge(pt_ready, i + 1)
                if i >= 2:
                    pe.wait_ge(att_copied, i - 1)
                for h in range(2):
                    o = bank[STAT if i % 2 == 0 else OUT][64 * h:64 * h + 64, :]
                    g = 2 * (i // 4) + h
                    v = [vtok[:, tb, g * 64:g * 64 + 64] for tb in range(2)]
                    pt = pt1[:, h, :]
                    pe.matmul(o[:, 0:P], v[0], pt[:, 0:P], start=True, stop=True)
                    pe.matmul(o[:, P:2 * P], v[0], pt[:, P:2 * P], start=True, stop=False)
                    ins = pe.matmul(o[:, P:2 * P], v[1], pt[:, 2 * P:3 * P], start=False, stop=True)
                ins.then_inc(att_out, 1)

            pe.wait_ge(summed, T0["qkv"] + 12)
            pe.wait_ge(scaled, SCALED["qkv"] + 12)
            pe.wait_ge(k_ready, 2)
            pe.wait_ge(v_ready, 1)
            scores1(0)
            for s in range(PAIRS1 + 2):
                if s >= 2:
                    turn1(s - 2)
                if s + 1 < PAIRS1:
                    scores1(s + 1)
                if s == 2:
                    pe.wait_ge(head_inv, 3)
                if s == PAIRS1 + 1:
                    first_body("wo", xb, None, att_lo, 0, [(0, 5, 3), (4, 5, 0), (4, 5, 1), (4, 5, 2)])
                if s >= 2:
                    values1(s - 2)
                if s == PAIRS1 - 1:
                    pe.wait_ge(masked, PAIRS1 - 1)
                    first_body("wo", xb, None, att_lo, 0, [(0, 4, 0), (0, 4, 1)])
                if s == PAIRS1:
                    pe.wait_ge(masked, PAIRS1)
                    first_body("wo", xb, None, att_lo, 0, [(0, 4, 2)])

            first_body("wo", xb, None, att_lo, 0, [(5, 6, p) for p in range(4)] + [(6, 8, p) for p in range(4)])
            rest("wo", xb)
            first_body("up1", xa, NORM["ffn1"], split_lo, SPLIT["ffn1"], STAIR)
            rest("up1", xa)
            gated_down("dn1", SPLIT["hid1"])

            def turn_v(t):
                pe.wait_ge(pool_scaled, t + 1)
                if t >= 1:
                    pe.wait_ge(v2_ready, t)
                for tb in range(2):
                    ins = pe.transpose(bank[STAT][:, tb * P:(tb + 1) * P], vfm[:, t % 2, tb * P:(tb + 1) * P],
                                       con("ident", P))
                ins.then_inc(v2_turned, 1)

            def scores2(i):
                h = PAIRS1 + i
                pe.wait_ge(roped, 8 + i + 1)
                if i >= 2:
                    pe.wait_ge(masked, h - 1)
                b = bank[ATT + i % 2]
                pe.matmul(b[:, 0:P], q2[:, i, 0:P], k2[:, i, 0:P], start=True, stop=True)
                pe.matmul(b[:, P:3 * P], q2[:, i, P:2 * P], k2[:, i, :], start=True, stop=True)\
                  .then_inc(scores, 1)

            def turn2(i):
                h = PAIRS1 + i
                pe.wait_ge(probs, i + 1)
                if i >= 1:
                    pe.wait_ge(pt_ready, h)
                else:
                    pe.wait_ge(v2_ready, 8)
                for j in range(3):
                    ins = pe.transpose(bank[STAT][:, j * P:(j + 1) * P], pr2[:, i % 2, j * P:(j + 1) * P],
                                       con("ident", P))
                ins.then_inc(pt_turned, 1)

            def values2(i):
                h = PAIRS1 + i
                pe.wait_ge(pt_ready, h + 1)
                if i >= 1:
                    pe.wait_ge(att_lo, h)
                o = bank[OUT]
                v = [vtok2[:, tb, i * HD2:(i + 1) * HD2] for tb in range(2)]
                pt = pt2[:, i % 2, :]
                pe.matmul(o[:, 0:P], v[0], pt[:, 0:P], start=True, stop=True)
                pe.matmul(o[:, P:2 * P], v[0], pt[:, P:2 * P], start=True, stop=False)
                pe.matmul(o[:, P:2 * P], v[1], pt[:, 2 * P:3 * P], start=False, stop=True).then_inc(att_out, 1)

            def beside(r):
                if 0 <= r - AT["v2"] - 1 < 8:
                    turn_v(r - AT["v2"] - 1)
                if head_of(r) is not None:
                    scores2(head_of(r))
                if head_of(r - 4) is not None:
                    turn2(head_of(r - 4))
                if head_of(r - 5) is not None:
                    values2(head_of(r - 5))

            first_body("x2", xa, NORM["pre2"], split_lo, SPLIT["pre2"], STAIR)
            for r in range(4, AT["ba"]):
                n = R0 + r
                pe.wait_ge(lo_ready, n + 1)
                if AT["rg"] <= r < AT["v2"]:
                    part = r - AT["rg"]
                    if part < 2:
                        pe.wait_ge(xc_lo, 4 * part + 4)
                    for m in range(4):
                        tile, t = T0["rg"] + 4 * part + m, 4 * (part % 2) + m
                        if part == 0:
                            pe.wait_ge(summed, tile - 3)
                        if part == 1:
                            pe.wait_ge(rstd_ready, NORM["pre2"] + 1)
                        if part >= 2:
                            pe.wait_ge(summed, tile - 7)
                        ins = blocks(r % 4, xb, [t // 2 * 2, t // 2 * 2 + 1], bank[4 * (part % 2) + m], True, True,
                                     at=2 * m)
                    ins.then_inc(piece_done, 1)
                else:
                    tile = T0[segment_of(r)] + r - AT[segment_of(r)]
                    early = AT["v2"] <= r < AT["v2"] + 4
                    pe.wait_ge(summed, tile - 7 if early else tile - 3)
                    blocks(r % 4, xa, range(8), bank[r % 4], True, True).then_inc(piece_done, 1)
                beside(r)

            first_body("ba", xb, None, att_lo, PAIRS1, IN_ORDER)
            rest("ba", xb)
            first_body("bl", xa, None, lru_lo, 0, STAIR)
            rest("bl", xa)
            first_body("out2", xb, None, mrg_lo, 0, STAIR)
            rest("out2", xb)
            keep_warm(3)
            stat(NORM["post2"])
            spread(NORM["post2"])
            keep_warm(4)
            first_body("mup", xa, NORM["mpre"], split_lo, SPLIT["mpre"], ONE_BY_ONE)
            rest("mup", xa)
            for q in range(32):
                g, c, m = q // 8, q // 2 % 4, q % 2
                n, tile = 4 * B0["mdn"] + q, T0["mdn"] + 2 * g + m
                pe.wait_ge(lo_ready, n + 1)
                if q in (0, 6):
                    pe.wait_ge(split_lo, SPLIT["hid2"] + (24 if q == 0 else 32))
                if c == 0:
                    pe.wait_ge(summed, tile - 3)
                blocks(n % 4, hid, range(8 * c, 8 * c + 8), bank[tile % 4], c == 0, c == 3)\
                    .then_inc(piece_done, 1)
            stat(NORM["mpost"])
            spread(NORM["mpost"])

        @block.scalar
        def _(act):
            def round_weights(b, p, kts=8, free=True):
                if free:
                    if p % 2 == 0:
                        act.wait_ge(raw_loaded[p // 2], 16 * b + 16)
                    act.wait_ge(piece_done, 4 * b + p - 3)
                slot = (b % 2) * 2 + p // 2
                src = raw[:, slot, (p % 2) * kts * P:(p % 2 + 1) * kts * P]
                act.activation(whi[:, p, 0:kts, :].rearrange("p k m -> p (k m)"), src, ACT.Copy)\
                   .then_inc(hi_ready, 1)

            def next_weights(n):
                if n + 4 < 4 * ALL_BODIES:
                    round_weights((n + 4) // 4, n % 4, blocks_of(n + 4))

            def spill_tile(n, tile, slot, at=0):
                act.wait_ge(piece_done, n + 1)
                if not isinstance(tile, int) or tile >= 4:
                    act.wait_ge(summed, tile - 3)
                act.activation(spill[:, slot, :], bank[at + slot][:, TOK:2 * TOK], ACT.Copy).then_inc(spilled, 1)

            def square(t, norm, src):
                if t >= 2:
                    act.wait_ge(sq_added, SQ0[norm] + max(1, t - 2))
                elif norm > 0 and t == 0:
                    act.wait_ge(sq_added, SQ0[norm])
                elif norm > 0:
                    act.wait_ge(stat_ready, norm)
                act.activation(sq[:, t % 2, :], src, ACT.Square).then_inc(squared, 1)

            def norm_tile(t, gain, norm, split_at):
                if norm > 0:
                    act.wait_ge(resid, RESID[norm] + t + 1)
                act.activation(xa[:, t, 0, :], x[:, t, :], ACT.Copy, scale=vec(gain, t)).then_inc(split_hi, 1)
                square(t, norm, x[:, t, :])

            def rms(norm):
                act.wait_ge(stat_ready, norm + 1)
                n, at = (2, SUMS) if norm in TURNED else (TOK, 0)
                act.activation(rstd[:, 0:n], bank[STAT][:, at:at + n], ACT.Sqrt, scale=1.0 / D, bias=EPS)\
                   .then_inc(rstd_ready, 1)

            def copy_spread(norm):
                act.wait_ge(spread_ready, TURNED[norm] + 1)
                act.activation(rbc[:], bank[STAT][:, 0:TOK], ACT.Copy).then_inc(rbc_ready, 1)

            act.wait_ge(warm_ready, 1)
            act.activation(scratch[:], pt1[:, 0, 0:1], ACT.Sqrt)
            act.wait_ge(vecs_loaded, 16)

            def first_tiles(tiles):
                for t in tiles:
                    act.activation(xa[:, t, 0, :], x[:, t, :], ACT.Copy, scale=vec("mix0", t)).then_inc(split_hi, 1)

            def first_squares(tiles):
                for t in tiles:
                    square(t, 0, x[:, t, :])
            act.wait_ge(x_loaded[0], 16)
            first_tiles(range(0, 4))
            act.wait_ge(first_raw[0], 16)
            round_weights(0, 0, free=False)
            first_squares(range(0, 2))
            act.wait_ge(raw_loaded[0], 16)
            round_weights(0, 1, free=False)
            act.wait_ge(x_loaded[1], 16)
            first_tiles(range(4, 8))
            first_squares(range(2, 4))
            act.wait_ge(first_raw[1], 16)
            round_weights(0, 2, free=False)
            first_squares(range(4, 6))
            act.wait_ge(raw_loaded[1], 16)
            round_weights(0, 3, free=False)
            first_squares(range(6, 8))

            def decay_constant(q):
                if q == 1:
                    act.wait_ge(lam_step, 2)
                    act.activation(lamb[:, 1, :], lamb[:, 0, :], ACT.Exp, scale=-1.0).then_inc(lam_act, 1)
                if q == 3:
                    act.wait_ge(lam_step, 3)
                    act.activation(lamb[:, 3, :], lamb[:, 2, :], ACT.Ln).then_inc(lam_act, 1)

            def first_tap(t):
                act.wait_ge(u_ready, t + 1)
                act.activation(cv[:, t, :], u[:, t, 0:TOK], ACT.Copy, scale=vec("conv", t)).then_inc(tap_ready, 1)

            def bx_step(i, p):
                n = 4 * (B0["bx"] + i) + p
                spill_tile(n, T0["bx"] + 4 * i + p, p)
                if i == 0 and p == 0:
                    rms(0)
                round_weights(B0["bx"] + i + 1, p)
                if i == 0 and p == 0:
                    copy_spread(0)
            for i in range(4):
                for p in range(4):
                    bx_step(i, p)
                    if i >= 1 and p % 2 == 1:
                        first_tap(2 * i - 2 + p // 2)

            for t in range(8):
                n = 4 * B0["c"] + t
                spill_tile(n, T0["c"] + t, t % 4)
                next_weights(n)
                if t < 2:
                    first_tap(6 + t)
                act.wait_ge(cy_ready, t + 1)
                act.activation(xb[:, t, 0, :], z[:, t % 4, :], ACT.Copy).then_inc(split_hi, 1)

            def residual_part(name, gain, norm, split_at):
                for t in range(8):
                    n = 4 * B0[name] + t
                    spill_tile(n, T0[name] + t, t % 4)
                    next_weights(n)
                    norm_tile(t, gain, norm, split_at)

            def gated_up(name, norm, layer):
                base = 22 * layer

                def body(i):
                    for p in range(4):
                        n = 4 * (B0[name] + i) + p
                        if isinstance(i, int) and i == 0 and p == 0:
                            rms(norm)
                        spill_tile(n, T0[name] + 4 * i + p, p)
                        round_weights(B0[name] + i + 1, p)
                        if p < 2:
                            act.wait_ge(scaled, SCALED[name] + 2 * i + p + 1)
                            act.wait_ge(gate_ready, base + 2 * i)
                            act.activation(act1[:, p, :], z[:, p, :], ACT.Silu).then_inc(silu_ready, 1)
                        else:
                            act.wait_ge(hval_ready, base + 2 * i + p - 1)
                            act.activation(hid[:, 2 * i + p - 2, 0, :], z[:, p, :], ACT.Copy).then_inc(split_hi, 1)
                body(0)
                repeat(act, 10, lambda i: body(i + 1))

            def gated_down(name, gain, norm, split_at):
                for q in range(24):
                    n = 4 * B0[name] + q
                    g, c, m = q // 6, q // 2 % 3, q % 2
                    t = 2 * g + m
                    if c == 2:
                        spill_tile(n, T0[name] + t, (T0[name] + t) % 4)
                    next_weights(n)
                    if name == "dn0":
                        decay_constant(q)
                    if c == 2:
                        norm_tile(t, gain, norm, split_at)

            residual_part("o", "ffn0", NORM["ffn0"], SPLIT["ffn0"])
            gated_up("up0", NORM["ffn0"], 0)
            gated_down("dn0", "mix1", NORM["mix1"], SPLIT["mix1"])

            for t in range(12):
                n = 4 * B0["qkv"] + t
                if t == 0:
                    rms(NORM["mix1"])
                spill_tile(n, T0["qkv"] + t, t % 4)
                if t < 11:
                    next_weights(n)
                if t not in (2, 3):
                    j = t if t < 2 else t - 2
                    act.wait_ge(scaled, SCALED["qkv"] + t + 1)
                    if j >= 2:
                        act.wait_ge(head_stat, j - 1)
                    else:
                        act.wait_ge(sq_added, SQ0[NORM["mix1"] + 1])
                    act.activation(sq[:, t % 2, :], qkv[:, t, :], ACT.Square).then_inc(head_sq, 1)
                if t == 11:
                    next_weights(n)
                if t == 6:
                    for j in range(2):
                        act.wait_ge(head_stat, j + 1)
                        act.activation(kstd[:, j, :], bank[ATT + j][:, 0:TOK], ACT.Sqrt, scale=1.0 / HD1, bias=EPS)\
                           .then_inc(head_std, 1)
                if t == 7:
                    act.wait_ge(v_turned, 1)
                    act.activation(vtok[:].rearrange("p a b -> p (a b)"), bank[OUT][:, :], ACT.Copy)\
                       .then_inc(v_ready, 1)
            act.wait_ge(head_stat, 10)
            act.activation(qstd[:], bank[STAT][:, TOK:TOK + 32], ACT.Sqrt, scale=1.0 / HD1, bias=EPS)\
               .then_inc(head_std, 1)

            def exps1(i):
                s = i % 2
                if i >= 2:
                    act.wait_ge(pt_turned, i - 1)
                act.wait_ge(negmax, i + 1)
                for b in range(2):
                    cols = slice(0, P) if b == 0 else slice(P, 3 * P)
                    for h in range(2):
                        j = 2 * b + h
                        act.activation(pr1[:, s, h, cols], sc1[:, s, h, cols], ACT.Exp, bias=nmx[:, s, j:j + 1],
                                       accum_out=den[:, s, j:j + 1])
                act.activation(esink[:, s, :], mx[:, s, :], ACT.Exp).then_inc(exped, 1)

            def copy_turned1(i):
                act.wait_ge(pt_turned, i + 1)
                if i >= 1:
                    act.wait_ge(att_out, i)
                for h in range(2):
                    ins = act.activation(pt1[:, h, :], bank[ATT + h][:, 0:3 * P], ACT.Copy)
                ins.then_inc(pt_ready, 1)

            for s in range(PAIRS1 + 3):
                if 2 <= s <= PAIRS1 + 1:
                    copy_turned1(s - 2)
                if s >= 3:
                    i = s - 3
                    act.wait_ge(att_out, i + 1)
                    if i >= 2:
                        act.wait_ge(att_lo, i - 1)
                    act.activation(z[:, i % 2, :], bank[STAT if i % 2 == 0 else OUT][:, 0:TOK], ACT.Copy)\
                       .then_inc(att_copied, 1)
                    act.wait_ge(att_copied, i + 1)
                    act.activation(xb[:, i, 0, :], z[:, i % 2, :], ACT.Copy).then_inc(att_hi, 1)
                if s < PAIRS1:
                    exps1(s)

            def exps(i, sc, pr):
                h, s = PAIRS1 + i, i % 2
                act.wait_ge(negmax, h + 1)
                if i >= 2:
                    act.wait_ge(pt_turned, h - 1)
                act.activation(pr[:, s, 0:P], sc[:, s, 0:P], ACT.Exp, bias=nmx[:, s, 0:1],
                               accum_out=den[:, s, 0:1])
                act.activation(pr[:, s, P:3 * P], sc[:, s, P:3 * P], ACT.Exp, bias=nmx[:, s, 1:2],
                               accum_out=den[:, s, 1:2]).then_inc(exped, 1)

            def copy_turned(i, pt):
                h = PAIRS1 + i
                act.wait_ge(pt_turned, h + 1)
                if i >= 2:
                    act.wait_ge(att_out, h - 1)
                act.activation(pt[:, i % 2, :], bank[STAT][:, 0:3 * P], ACT.Copy).then_inc(pt_ready, 1)

            residual_part("wo", "ffn1", NORM["ffn1"], SPLIT["ffn1"])
            gated_up("up1", NORM["ffn1"], 1)
            gated_down("dn1", "pre2", NORM["pre2"], SPLIT["pre2"])

            def beside(r):
                if 0 <= r - CONV_AT < 16:
                    t = (r - CONV_AT) // 2
                    if r % 2 == 0:
                        act.wait_ge(scaled, SCALED["x2"] + t + 1)
                        act.wait_ge(pad2_ready, 1)
                        act.activation(xc[:, t, :], xl[:, t, 0:TOK], ACT.Identity, scale=vec("conv2", t),
                                       bias=vec("convb2", t)).then_inc(tap0, 1)
                    if r % 2 == 0 and t >= 1:
                        act.wait_ge(taps, 3 * t)
                        act.activation(xb[:, t - 1, 0, :], xc[:, t - 1, :], ACT.Copy).then_inc(xc_hi, 1)
                if r == CONV_AT + 16:
                    act.wait_ge(taps, 24)
                    act.activation(xb[:, 7, 0, :], xc[:, 7, :], ACT.Copy).then_inc(xc_hi, 1)
                for first, at in ((0, AT["q2"] + 1), (8, AT["k2"] + 1)):
                    if 0 <= r - at < 8:
                        j = first + r - at
                        src, t = (q2, j) if j < 8 else (k2, j - 8)
                        act.wait_ge(scaled, SCALED["q2" if j < 8 else "k2"] + t + 1)
                        act.wait_ge(pad2_ready, 1)
                        if j >= 2:
                            act.wait_ge(roped, j - 1)
                        act.activation(rtmp[0:16, j % 2, 1, :], src[32:48, t, :], ACT.Copy)
                        act.activation(rtmp[32:48, j % 2, 1, :], src[0:16, t, :], ACT.Copy).then_inc(rot_out, 1)
                if 0 <= r - AT["v2"] - 1 < 8:
                    t = r - AT["v2"] - 1
                    act.wait_ge(v2_turned, t + 1)
                    act.activation(vtok2[:, :, t * P:(t + 1) * P],
                                   bank[STAT][:, 0:TOK].rearrange("p (a b) -> p a b", a=2), ACT.Copy)\
                       .then_inc(v2_ready, 1)
                if 0 <= r - AT["v2"] < 16:
                    t, odd = divmod(r - AT["v2"], 2)
                    if not odd:
                        if t == 0:
                            act.wait_ge(lam_step, 10)
                            act.wait_ge(r_ready, 2)
                        if t >= 2:
                            act.wait_ge(m_step, t - 1)
                        act.activation(gate[:, t % 2, :], rr[:, t, :], ACT.Tanh, scale=lam8[:, t:t + 1])
                        act.activation(rr[:, t, :], rr[:, t, :], ACT.Exp, scale=nlam8[:, t:t + 1]).then_inc(a_ready, 1)
                    else:
                        act.wait_ge(a_ready, t + 1)
                        act.activation(sq[:, t % 2, :], rr[:, t, :], ACT.Square).then_inc(a2_ready, 1)
                if r - AT["v2"] in (16, 17):
                    half = slice(0, 6) if r == AT["v2"] + 16 else slice(6, KT)
                    act.wait_ge(m_step, 6 if r == AT["v2"] + 16 else KT)
                    act.activation(xl[:, half, 0:TOK], xl[:, half, 0:TOK], ACT.Sqrt).then_inc(mult_ready, 1)
                if head_of(r - 5) is not None:
                    i = head_of(r - 5)
                    act.wait_ge(att_out, PAIRS1 + i + 1)
                    act.activation(xb[:, i, 0, :], bank[OUT][:, 0:TOK], ACT.Copy).then_inc(att_hi, 1)
                if head_of(r - 1) is not None:
                    exps(head_of(r - 1), sc2, pr2)
                if head_of(r - 4) is not None:
                    copy_turned(head_of(r - 4), pt2)
                if r == AT["v2"] + 28:
                    act.wait_ge(pool_scaled, POOL_SCALED["g2"] + 8)
                    act.activation(g2[:], g2[:], ACT.Gelu_apprx_tanh).then_inc(gelu_ready, 1)
                if r == AT["ba"] - 1:
                    act.wait_ge(pool_scaled, POOL_SCALED["ga"] + 8)
                    act.activation(ga[:], ga[:], ACT.Sigmoid).then_inc(gates_ready, 1)

            for r in range(AT["ba"]):
                n = R0 + r
                if AT["rg"] <= r < AT["v2"]:
                    part = r - AT["rg"]
                    for m in range(4):
                        spill_tile(n, T0["rg"] + 4 * part + m, m, 4 * (part % 2))
                    next_weights(n)
                    act.wait_ge(summed, T0["rg"] + 4 * part + 4)
                    half = slice(4 * (part % 2), 4 * (part % 2) + 4)
                    act.activation((rr if part < 2 else ga)[:, half, :], z[:, :, :], ACT.Sigmoid)\
                       .then_inc(r_ready if part < 2 else i_ready, 1)
                else:
                    if r == 0:
                        rms(NORM["pre2"])
                    spill_tile(n, T0[segment_of(r)] + r - AT[segment_of(r)], r % 4)
                    next_weights(n)
                beside(r)
            for t in range(8):
                n = 4 * B0["ba"] + t
                spill_tile(n, T0["ba"] + t, t % 4)
                next_weights(n)
                for k in range(t - 1, t if t < 7 else 8):
                    if k >= 0:
                        act.wait_ge(lru_ready, k + 1)
                        act.activation(xa[:, k, 0, :], xc[:, k, :], ACT.Copy).then_inc(lru_hi, 1)
                if t == 1:
                    act.wait_ge(pool_scaled, POOL_SCALED["gl"] + 8)
                    act.activation(gl[:], gl[:], ACT.Sigmoid).then_inc(gates_ready, 1)
            def merged_hi(t):
                act.wait_ge(merged, t + 1)
                act.activation(xb[:, t, 0, :], z[:, t % 4, :], ACT.Copy).then_inc(mrg_hi, 1)

            for t in range(8):
                n = 4 * B0["bl"] + t
                spill_tile(n, T0["bl"] + t, t % 4)
                next_weights(n)
                if t >= 1:
                    merged_hi(t - 1)
            merged_hi(7)
            for t in range(8):
                n = 4 * B0["out2"] + t
                spill_tile(n, T0["out2"] + t, t % 4)
                if t < 7:
                    next_weights(n)
                act.wait_ge(summed, T0["out2"] + t + 1)
                square(t, NORM["post2"], mix[:, t, :])
                if t == 7:
                    rms(NORM["post2"])
                if t == 5:
                    act.activation(scratch[:], con("ones", 1), ACT.Sqrt)
                if t == 7:
                    next_weights(n)
            copy_spread(NORM["post2"])
            for t in range(8):
                norm_tile(t, "mpre", NORM["mpre"], SPLIT["mpre"])

            def up_hi(tile, slot):
                act.wait_ge(sqrelu_ready, tile + 1)
                act.activation(hid[:, tile, 0, :], z[:, slot, :], ACT.Copy).then_inc(split_hi, 1)

            def squared_up(i):
                for p in range(4):
                    if isinstance(i, int) and i == 0 and p == 0:
                        rms(NORM["mpre"])
                    spill_tile(4 * (B0["mup"] + i) + p, T0["mup"] + 4 * i + p, p)
                    round_weights(B0["mup"] + i + 1, p)
                    if isinstance(i, int) and i == 0 and p == 0:
                        copy_spread(NORM["mpre"])
                    if p > 0 or not isinstance(i, int):
                        up_hi(4 * i + p - 1, (p - 1) % 4)
            squared_up(0)
            repeat(act, 7, lambda i: squared_up(i + 1))
            up_hi(31, 3)
            for q in range(32):
                n = 4 * B0["mdn"] + q
                t = 2 * (q // 8) + q % 2
                if q // 2 % 4 == 3:
                    spill_tile(n, T0["mdn"] + t, (T0["mdn"] + t) % 4)
                next_weights(n)
                if q // 2 % 4 == 3:
                    act.wait_ge(summed, T0["mdn"] + t + 1)
                    square(t, NORM["mpost"], mres[:, t, :])
                    if t >= 6:
                        act.wait_ge(squared, 8 * NORM["mpost"] + t + 1)
                        act.activation(mres[:, t, :], mres[:, t, :], ACT.Copy, scale=vec("mpost", t))\
                           .then_inc(gained, 1)
            rms(NORM["mpost"])
            copy_spread(NORM["mpost"])

        @block.vector
        def _(dve):
            def rest_weights(b, p, kts=8, free=True):
                dve.wait_ge(hi_ready, 4 * b + p + 1)
                if free:
                    dve.wait_ge(piece_done, 4 * b + p - 3)
                slot = (b % 2) * 2 + p // 2
                src = raw[:, slot, (p % 2) * kts * P:(p % 2 + 1) * kts * P]
                dve.tensor_tensor(wlo[:, p, 0:kts, :].rearrange("p k m -> p (k m)"), src,
                                  whi[:, p, 0:kts, :].rearrange("p k m -> p (k m)").bitcast(F32), ALU.subtract)\
                   .then_inc(lo_ready, 1)

            def next_weights(n):
                if n + 4 < 4 * ALL_BODIES:
                    rest_weights((n + 4) // 4, n % 4, blocks_of(n + 4))

            def sum_tile(tile, slot, dst=None):
                dve.wait_ge(spilled, tile + 1)
                dve.tensor_tensor(z[:, slot, :] if dst is None else dst, bank[slot][:, 0:TOK], spill[:, slot, :],
                                  ALU.add)\
                   .then_inc(summed, 1)

            def scale_tile(tile, slot, dst=None):
                dve.wait_ge(summed, tile + 1)
                dve.tensor_tensor(z[:, slot, :] if dst is None else dst, z[:, slot, :], rbc[:], ALU.mult)\
                   .then_inc(scaled, 1)

            def rms(norm):
                dve.wait_ge(rstd_ready, norm + 1)
                if norm in TURNED:
                    dve.reciprocal(rinv[:], rstd[:, 0:2]).then_inc(rinv_ready, 1)
                else:
                    dve.reciprocal(rbc[:], rstd[:]).then_inc(rbc_ready, 1)
                    dve.wait_ge(rbc_ready, norm + 1)

            def norm_lo(t, gain, split_at):
                dve.wait_ge(split_hi, split_at + t + 1)
                dve.scalar_tensor_tensor(out=xa[:, t, 1, :], in0=x[:, t, :], scalar=vec(gain, t),
                                         in1=xa[:, t, 0, :].bitcast(F32), op0=ALU.mult, op1=ALU.subtract)\
                   .then_inc(split_lo, 1)

            dve.memset(pt1[:], 0.0).then_inc(warm_ready, 1)
            dve.memset(u[:, :, 0:2], 0.0).then_inc(pad_ready, 1)
            dve.wait_ge(vecs_loaded, 16)
            dve.scalar_tensor_tensor(out=kgain[:], in0=vec("qg", 0), scalar=HD1 ** -0.5, in1=vec("kg", 0),
                                     op0=ALU.mult, op1=ALU.mult).then_inc(kgain_ready, 1)
            for t in range(KT):
                if t % 4 == 0:
                    dve.wait_ge(x_loaded[t // 4], 16)
                norm_lo(t, "mix0", SPLIT["mix0"])
                if t == 3:
                    rest_weights(0, 0, free=False)
                    rest_weights(0, 1, free=False)
            rest_weights(0, 2, free=False)
            rest_weights(0, 3, free=False)

            def decay_constant(q):
                lam = vecs[:, VEC["lam"]:VEC["lam"] + KT]
                L = [lamb[:, i, :] for i in range(6)]
                if q == 0:
                    dve.tensor_scalar(L[5], lam, -1.0, None, ALU.mult).then_inc(lam_step, 1)
                    dve.wait_ge(lam_step, 1)
                    dve.tensor_tensor(L[0], lam, L[5], ALU.max).then_inc(lam_step, 1)
                if q == 2:
                    dve.wait_ge(lam_act, 1)
                    dve.tensor_scalar(L[2], L[1], 1.0, None, ALU.add).then_inc(lam_step, 1)
                    dve.wait_ge(lam_step, 3)
                    dve.tensor_scalar(L[4], L[2], -1.0, 1e-30, ALU.add, ALU.max).then_inc(lam_step, 1)
                    dve.wait_ge(lam_step, 4)
                    dve.reciprocal(L[0], L[4]).then_inc(lam_step, 1)
                if q == 4:
                    dve.wait_ge(lam_step, 5)
                    dve.wait_ge(lam_act, 2)
                    dve.tensor_tensor(L[4], L[3], L[0], ALU.mult).then_inc(lam_step, 1)
                    dve.wait_ge(lam_step, 6)
                    dve.scalar_tensor_tensor(out=L[4], in0=L[2], scalar=1.0, in1=L[4], op0=ALU.is_equal,
                                             op1=ALU.add).then_inc(lam_step, 1)
                    dve.wait_ge(lam_step, 7)
                    dve.tensor_tensor(L[4], L[4], L[1], ALU.mult).then_inc(lam_step, 1)
                    dve.wait_ge(lam_step, 8)
                    dve.scalar_tensor_tensor(out=L[3], in0=L[5], scalar=0.0, in1=L[4], op0=ALU.max,
                                             op1=ALU.add).then_inc(lam_step, 1)
                    dve.wait_ge(lam_step, 9)
                    dve.tensor_scalar(lam8[:], L[3], 8.0, None, ALU.mult)
                    dve.tensor_scalar(nlam8[:], L[3], -8.0, None, ALU.mult).then_inc(lam_step, 1)
                if q == 5:
                    dve.wait_ge(small_in, 32)
                    dve.tensor_scalar(nsinks[:], sinks[:], -1.0, None, ALU.mult).then_inc(nsinks_ready, 1)

            def bx_step(i, p):
                tile = T0["bx"] + 4 * i + p
                if i >= 1:
                    dve.wait_ge(u_ready, 2 * i)
                sum_tile(tile, p)
                if i == 0 and p == 0:
                    rms(0)
                    rest_weights(B0["bx"] + i + 1, p)
                    dve.wait_ge(rbc_ready, 1)
                    scale_tile(tile, p)
                else:
                    scale_tile(tile, p)
                    rest_weights(B0["bx"] + i + 1, p)
            def conv_taps(t0):
                for tap in (1, 2):
                    for t in (t0, t0 + 1):
                        if tap == 1:
                            dve.wait_ge(tap_ready, t + 1)
                        else:
                            dve.wait_ge(conv_step, 2 * t0 + 1 + t - t0)
                        dve.scalar_tensor_tensor(out=cv[:, t, :], in0=u[:, t, tap:TOK + tap],
                                                 scalar=vec("conv", 8 * tap + t), in1=cv[:, t, :],
                                                 op0=ALU.mult, op1=ALU.add).then_inc(conv_step, 1)
            for i in range(4):
                for p in range(4):
                    bx_step(i, p)
                if i >= 1:
                    conv_taps(2 * i - 2)

            def split_lo_z(t):
                dve.wait_ge(cy_ready, t + 1)
                dve.wait_ge(split_hi, SPLIT["cy"] + t + 1)
                dve.tensor_tensor(xb[:, t, 1, :], z[:, t % 4, :], xb[:, t, 0, :].bitcast(F32), ALU.subtract)\
                   .then_inc(split_lo, 1)

            for t in range(8):
                tile = T0["c"] + t
                if t == 0:
                    dve.wait_ge(u_ready, 8)
                sum_tile(tile, t % 4)
                dve.wait_ge(summed, tile + 1)
                dve.wait_ge(cv_ready, t + 1)
                dve.tensor_tensor(z[:, t % 4, :], z[:, t % 4, :], cv[:, t, :], ALU.mult).then_inc(cy_ready, 1)
                next_weights(4 * B0["c"] + t)
                split_lo_z(t)
                if t == 1:
                    conv_taps(6)

            def add_residual(t, tile, norm):
                dve.wait_ge(summed, tile + 1)
                dve.tensor_tensor(x[:, t, :], x[:, t, :], z[:, tile % 4, :], ALU.add).then_inc(resid, 1)

            def residual_part(name, gain, norm, split_at):
                for t in range(8):
                    tile = T0[name] + t
                    sum_tile(tile, tile % 4)
                    add_residual(t, tile, norm)
                    next_weights(4 * B0[name] + t)
                    norm_lo(t, gain, split_at)

            def gated_up(name, norm, layer):
                base = 22 * layer
                split_at = SPLIT["hid0"] if layer == 0 else SPLIT["hid1"]

                def body(i):
                    for p in range(4):
                        tile = T0[name] + 4 * i + p
                        if isinstance(i, int) and i == 0 and p == 0:
                            rms(norm)
                        if p < 2 and not (isinstance(i, int) and base + 2 * i == 0):
                            dve.wait_ge(silu_ready, base + 2 * i)
                        sum_tile(tile, p)
                        if p < 2:
                            scale_tile(tile, p)
                        else:
                            dve.wait_ge(summed, tile + 1)
                            dve.wait_ge(gate_ready, base + 2 * i + p - 1)
                            dve.tensor_tensor(z[:, p, :], z[:, p, :], gate[:, p - 2, :], ALU.mult)\
                               .then_inc(hval_ready, 1)
                        rest_weights(B0[name] + i + 1, p)
                    for m in range(2):
                        dve.wait_ge(split_hi, split_at + 2 * i + m + 1)
                        dve.tensor_tensor(hid[:, 2 * i + m, 1, :], z[:, 2 + m, :],
                                          hid[:, 2 * i + m, 0, :].bitcast(F32), ALU.subtract)\
                           .then_inc(split_lo, 1)
                body(0)
                repeat(dve, 10, lambda i: body(i + 1))

            def gated_down(name, gain, norm, split_at):
                for q in range(24):
                    g, c, m = q // 6, q // 2 % 3, q % 2
                    t = 2 * g + m
                    tile = T0[name] + t
                    if c == 2:
                        sum_tile(tile, tile % 4)
                        add_residual(t, tile, norm)
                    next_weights(4 * B0[name] + q)
                    if name == "dn0":
                        decay_constant(q)
                    if c == 2:
                        norm_lo(t, gain, split_at)

            residual_part("o", "ffn0", NORM["ffn0"], SPLIT["ffn0"])
            gated_up("up0", NORM["ffn0"], 0)
            gated_down("dn0", "mix1", NORM["mix1"], SPLIT["mix1"])

            for t in range(12):
                tile = T0["qkv"] + t
                if t == 0:
                    rms(NORM["mix1"])
                sum_tile(tile, t % 4)
                scale_tile(tile, t % 4, qkv[:, t, :])
                if t < 11:
                    next_weights(4 * B0["qkv"] + t)
                if t in (6, 7):
                    j = t - 6
                    dve.wait_ge(head_std, j + 1)
                    dve.reciprocal(kinv[:, j, :], kstd[:, j, :]).then_inc(head_inv, 1)
                    dve.wait_ge(head_inv, j + 1)
                    dve.wait_ge(kgain_ready, 1)
                    dve.scalar_tensor_tensor(out=qkv[:, j, :], in0=qkv[:, j, :], scalar=kgain[:], in1=kinv[:, j, :],
                                             op0=ALU.mult, op1=ALU.mult).then_inc(k_ready, 1)
            dve.wait_ge(head_std, 3)
            dve.reciprocal(rq[:], qstd[:]).then_inc(head_inv, 1)
            dve.wait_ge(head_inv, 3)
            dve.wait_ge(bias_in, 16)
            dve.wait_ge(nsinks_ready, 1)

            def mask1(i):
                s = i % 2
                dve.wait_ge(scores, i + 1)
                if i >= 2:
                    dve.wait_ge(exped, i - 1)
                for b in range(2):
                    cols = slice(0, P) if b == 0 else slice(P, 3 * P)
                    for h in range(2):
                        j = 4 * i + 2 * b + h
                        ins = dve.scalar_tensor_tensor(out=sc1[:, s, h, cols], in0=bank[2 * s + h][:, cols],
                                                       scalar=rq[:, j:j + 1], in1=bias[:, 2 * i + h, cols],
                                                       op0=ALU.mult, op1=ALU.add)
                ins.then_inc(masked, 1)
                if i >= 1:
                    dve.wait_ge(exped, i)
                    dve.tensor_tensor(den[:, 1 - s, :], den[:, 1 - s, :], esink[:, 1 - s, :], ALU.add)\
                       .then_inc(den_step, 1)
                dve.wait_ge(masked, i + 1)
                dve.tensor_reduce(mx[:, s, 0:2], sc1[:, s, :, 0:P], AX.X, ALU.max)
                if i >= 1:
                    dve.wait_ge(den_step, 2 * i - 1)
                    dve.reciprocal(rden[:, 1 - s, :], den[:, 1 - s, :]).then_inc(den_step, 1)
                dve.tensor_reduce(mx[:, s, 2:4], sc1[:, s, :, P:3 * P], AX.X, ALU.max).then_inc(maxed, 1)
                dve.wait_ge(maxed, i + 1)
                dve.scalar_tensor_tensor(out=nmx[:, s, :], in0=mx[:, s, :], scalar=-1.0,
                                         in1=nsinks[:, 4 * i:4 * i + 4], op0=ALU.mult, op1=ALU.min)\
                   .then_inc(nmx_ready, 1)
                dve.wait_ge(nmx_ready, i + 1)
                dve.tensor_tensor(mx[:, s, :], nmx[:, s, :], sinks[:, 4 * i:4 * i + 4], ALU.add).then_inc(negmax, 1)

            def denominators(i):
                s = i % 2
                dve.wait_ge(exped, i + 1)
                dve.tensor_tensor(den[:, s, :], den[:, s, :], esink[:, s, :], ALU.add).then_inc(den_step, 1)
                dve.wait_ge(den_step, 2 * i + 1)
                dve.reciprocal(rden[:, s, :], den[:, s, :]).then_inc(den_step, 1)

            for s in range(PAIRS1):
                mask1(s)
                if s == 0:
                    next_weights(4 * B0["qkv"] + 11)
            denominators(PAIRS1 - 1)

            residual_part("wo", "ffn1", NORM["ffn1"], SPLIT["ffn1"])
            gated_up("up1", NORM["ffn1"], 1)
            gated_down("dn1", "pre2", NORM["pre2"], SPLIT["pre2"])

            dve.memset(rtmp[:], 0.0)
            dve.memset(xl[:, :, 0:3], 0.0).then_inc(pad2_ready, 1)

            def mask2(i):
                s, h = i % 2, PAIRS1 + i
                dve.wait_ge(scores, h + 1)
                if i >= 2:
                    dve.wait_ge(exped, h - 1)
                dve.scalar_tensor_tensor(out=sc2[:, s, :], in0=bank[ATT + s][:, 0:3 * P], scalar=HD2 ** -0.5,
                                         in1=con("mask", 3 * P), op0=ALU.mult, op1=ALU.add).then_inc(masked, 1)
                dve.wait_ge(masked, h + 1)
                dve.tensor_reduce(mx[:, s, 0:1], sc2[:, s, 0:P], AX.X, ALU.max)
                dve.tensor_reduce(mx[:, s, 1:2], sc2[:, s, P:3 * P], AX.X, ALU.max).then_inc(maxed, 1)
                dve.wait_ge(maxed, h + 1)
                dve.tensor_scalar(nmx[:, s, :], mx[:, s, :], -1.0, None, ALU.mult).then_inc(negmax, 1)

            def normalise2(i):
                s, h = i % 2, PAIRS1 + i
                dve.wait_ge(exped, h + 1)
                dve.reciprocal(rden[:, s, :], den[:, s, :]).then_inc(den_step, 1)
                dve.wait_ge(den_step, 2 * PAIRS1 + i + 1)
                dve.tensor_scalar(pr2[:, s, 0:P], pr2[:, s, 0:P], rden[:, s, 0:1], None, ALU.mult)
                dve.tensor_scalar(pr2[:, s, P:3 * P], pr2[:, s, P:3 * P], rden[:, s, 1:2], None, ALU.mult)\
                   .then_inc(probs, 1)

            def xc_split(t):
                dve.wait_ge(xc_hi, t + 1)
                dve.tensor_tensor(xb[:, t, 1, :], xc[:, t, :], xb[:, t, 0, :].bitcast(F32), ALU.subtract)\
                   .then_inc(xc_lo, 1)

            def beside(r):
                if 0 <= r - CONV_AT < 17:
                    t, odd = divmod(r - CONV_AT, 2)
                    if not odd and t >= 1:
                        xc_split(t - 1)
                    for j in ((2, 3) if odd else (1,)):
                        if t == KT:
                            break
                        if j == 1:
                            dve.wait_ge(tap0, t + 1)
                        else:
                            dve.wait_ge(taps, 3 * t + j - 1)
                        dve.scalar_tensor_tensor(out=xc[:, t, :], in0=xl[:, t, j:j + TOK],
                                                 scalar=vec("conv2", 8 * j + t), in1=xc[:, t, :],
                                                 op0=ALU.mult, op1=ALU.add).then_inc(taps, 1)
                if 0 <= r - AT["v2"] - 2 < 16 and (r - AT["v2"]) % 2 == 0:
                    t = (r - AT["v2"] - 2) // 2
                    dve.wait_ge(a2_ready, t + 1)
                    dve.scalar_tensor_tensor(out=xl[:, t, 0:TOK], in0=sq[:, t % 2, :], scalar=1.0,
                                             in1=gate[:, t % 2, :], op0=ALU.add, op1=ALU.mult).then_inc(m_step, 1)
                if 0 <= r - AT["v2"] - 20 < 8:
                    t = r - AT["v2"] - 20
                    dve.wait_ge(bx_ready, t + 1)
                    dve.wait_ge(a_ready, t + 1)
                    dve.tensor_tensor_scan(xc[:, t, :], rr[:, t, :], xl[:, t, 0:TOK], 0.0, ALU.mult, ALU.add)\
                       .then_inc(scanned, 1)
                if head_of(r) is not None:
                    mask2(head_of(r))
                if head_of(r - 2) is not None:
                    normalise2(head_of(r - 2))
                if head_of(r - 5) is not None:
                    i = head_of(r - 5)
                    dve.wait_ge(att_hi, PAIRS1 + i + 1)
                    dve.tensor_tensor(xb[:, i, 1, :], bank[OUT][:, 0:TOK], xb[:, i, 0, :].bitcast(F32),
                                      ALU.subtract).then_inc(att_lo, 1)

            for r in range(AT["ba"]):
                n = R0 + r
                name = segment_of(r)
                if name == "rg":
                    part = r - AT["rg"]
                    if part == 0:
                        dve.wait_ge(scaled, SCALED["k2"] + 8)
                    for m in range(4):
                        if part == 1 or part == 2:
                            dve.wait_ge(r_ready, part)
                        if part == 3:
                            dve.wait_ge(i_ready, 1)
                        dve.wait_ge(spilled, T0["rg"] + 4 * part + m + 1)
                        dve.scalar_tensor_tensor(out=z[:, m, :], in0=bank[4 * (part % 2) + m][:, 0:TOK],
                                                 scalar=vec("ba" if part < 2 else "bi", 4 * (part % 2) + m),
                                                 in1=spill[:, m, :], op0=ALU.add, op1=ALU.add).then_inc(summed, 1)
                    next_weights(n)
                else:
                    t = r - AT[name]
                    tile = T0[name] + t
                    if name == "ga" and t == 0:
                        dve.wait_ge(ix_ready, KT)
                    if name in POOL_SCALED:
                        if name == "v2":
                            if t >= 2:
                                dve.wait_ge(v2_turned, t - 1)
                            dst = vfm[:, t % 2, :]
                        else:
                            dst = DST[name][:, t, :]
                        sum_tile(tile, r % 4, dst)
                    else:
                        if r == 0:
                            rms(NORM["pre2"])
                        sum_tile(tile, r % 4)
                        scale_tile(tile, r % 4, xl[:, t, 3:TOK + 3] if name == "x2" else DST[name][:, t, :])
                    next_weights(n)
                beside(r)

            for t in range(8):
                tile = T0["ba"] + t
                sum_tile(tile, t % 4)
                dve.wait_ge(summed, tile + 1)
                dve.wait_ge(gates_ready, 1)
                dve.tensor_tensor(ga[:, t, :], ga[:, t, :], z[:, t % 4, :], ALU.mult).then_inc(gated_att, 1)
                next_weights(4 * B0["ba"] + t)
                for k in range(t - 1, t if t < 7 else 8):
                    if k >= 0:
                        dve.wait_ge(lru_hi, k + 1)
                        dve.tensor_tensor(xa[:, k, 1, :], xc[:, k, :], xa[:, k, 0, :].bitcast(F32), ALU.subtract)\
                           .then_inc(lru_lo, 1)

            def merged_lo(t):
                dve.wait_ge(mrg_hi, t + 1)
                dve.tensor_tensor(xb[:, t, 1, :], z[:, t % 4, :], xb[:, t, 0, :].bitcast(F32), ALU.subtract)\
                   .then_inc(mrg_lo, 1)

            dve.wait_ge(gates_ready, 2)
            for t in range(8):
                tile = T0["bl"] + t
                sum_tile(tile, t % 4)
                dve.wait_ge(summed, tile + 1)
                dve.tensor_tensor(z[:, t % 4, :], z[:, t % 4, :], gl[:, t, :], ALU.mult).then_inc(gated_lru, 1)
                next_weights(4 * B0["bl"] + t)
                if t >= 1:
                    merged_lo(t - 1)
            merged_lo(7)

            for t in range(8):
                sum_tile(T0["out2"] + t, t % 4, mix[:, t, :])
                if t == 7:
                    rms(NORM["post2"])
                next_weights(4 * B0["out2"] + t)

            def post_scaled(src, gain, t, done, base):
                if t >= 2:
                    dve.wait_ge(done, base + t - 1)
                dve.scalar_tensor_tensor(out=z[:, t % 2, :], in0=src[:, t, :], scalar=vec(gain, t), in1=rbc[:],
                                         op0=ALU.mult, op1=ALU.mult).then_inc(post_step, 1)

            def post_add(t, at, done):
                dve.wait_ge(post_step, at + t + 1)
                dve.tensor_tensor(x[:, t, :], x[:, t, :], z[:, t % 2, :], ALU.add).then_inc(done, 1)

            dve.wait_ge(rbc_ready, NORM["post2"] + 1)
            post_scaled(mix, "post2", 0, resid, RESID[6])
            for t in range(8):
                if t < 7:
                    post_scaled(mix, "post2", t + 1, resid, RESID[6])
                post_add(t, 0, resid)
                if t >= 1:
                    norm_lo(t - 1, "mpre", SPLIT["mpre"])
            dve.wait_ge(resid, RESID[6] + 8)
            norm_lo(7, "mpre", SPLIT["mpre"])

            def up_lo(tile, slot):
                dve.wait_ge(split_hi, SPLIT["hid2"] + tile + 1)
                dve.tensor_tensor(hid[:, tile, 1, :], z[:, slot, :], hid[:, tile, 0, :].bitcast(F32),
                                  ALU.subtract).then_inc(split_lo, 1)

            def squared_up(i):
                for p in range(4):
                    tile = T0["mup"] + 4 * i + p
                    if isinstance(i, int) and i == 0 and p == 0:
                        rms(NORM["mpre"])
                    sum_tile(tile, p)
                    dve.wait_ge(summed, tile + 1)
                    dve.scalar_tensor_tensor(out=z[:, p, :], in0=z[:, p, :], scalar=0.0, in1=z[:, p, :],
                                             op0=ALU.max, op1=ALU.mult).then_inc(relu_ready, 1)
                    rest_weights(B0["mup"] + i + 1, p)
                    if isinstance(i, int) and i == 0 and p == 0:
                        dve.wait_ge(rbc_ready, NORM["mpre"] + 1)
                        dve.tensor_tensor(rbc2[:], rbc[:], rbc[:], ALU.mult).then_inc(rbc2_ready, 1)
                    if p > 0 or not isinstance(i, int):
                        up_lo(4 * i + p - 1, (p - 1) % 4)
            squared_up(0)
            repeat(dve, 7, lambda i: squared_up(i + 1))
            up_lo(31, 3)
            for q in range(32):
                t = 2 * (q // 8) + q % 2
                if q // 2 % 4 == 3:
                    sum_tile(T0["mdn"] + t, (T0["mdn"] + t) % 4, mres[:, t, :])
                next_weights(4 * B0["mdn"] + q)
            rms(NORM["mpost"])
            dve.wait_ge(rbc_ready, NORM["mpost"] + 1)
            post_scaled(mres, "mpost", 0, final, 0)
            for t in range(6):
                if t < 5:
                    post_scaled(mres, "mpost", t + 1, final, 0)
                post_add(t, 8, final)

        @block.gpsimd
        def _(pool):
            def add_squares(norm):
                for t in range(1, 7 if norm in TURNED else 8):
                    pool.wait_ge(squared, 8 * norm + t + 1)
                    if t == 1:
                        if norm > 0:
                            pool.wait_ge(stat_ready, norm)
                        pool.tensor_tensor(ssum[:], sq[:, 0, :], sq[:, 1, :], ALU.add).then_inc(sq_added, 1)
                    else:
                        pool.wait_ge(sq_added, SQ0[norm] + t - 1)
                        pool.tensor_tensor(ssum[:], ssum[:], sq[:, t % 2, :], ALU.add).then_inc(sq_added, 1)

            def gates(name, norm, layer):
                base = 22 * layer
                pool.wait_ge(rbc_ready, norm + 1)

                def body(i):
                    for m in range(2):
                        pool.wait_ge(silu_ready, base + 2 * i + m + 1)
                        if not isinstance(i, int) or base:
                            pool.wait_ge(hval_ready, base + 2 * i)
                        pool.tensor_tensor(gate[:, m, :], act1[:, m, :], rbc[:], ALU.mult).then_inc(gate_ready, 1)
                body(0)
                repeat(pool, 10, lambda i: body(i + 1))

            add_squares(0)
            pool.wait_ge(pad_ready, 1)

            def products(i):
                for m in range(2):
                    pool.wait_ge(scaled, 4 * i + 3 + m)
                    pool.tensor_tensor(u[:, 2 * i + m, 2:TOK + 2], z[:, m, :], z[:, 2 + m, :], ALU.mult)\
                        .then_inc(u_ready, 1)

            def scaled_conv(t0):
                for t in (t0, t0 + 1):
                    pool.wait_ge(conv_step, 2 * t0 + 3 + t - t0)
                    pool.tensor_tensor(cv[:, t, :], cv[:, t, :], rbc[:], ALU.mult).then_inc(cv_ready, 1)
            for i in range(4):
                products(i)
                if i >= 2:
                    scaled_conv(2 * i - 4)
            scaled_conv(4)
            scaled_conv(6)
            add_squares(NORM["ffn0"])
            gates("up0", NORM["ffn0"], 0)
            add_squares(NORM["mix1"])
            def attention_lo(i):
                pool.wait_ge(att_hi, i + 1)
                pool.tensor_tensor(xb[:, i, 1, :], z[:, i % 2, :], xb[:, i, 0, :].bitcast(F32), ALU.subtract)\
                    .then_inc(att_lo, 1)

            for i in range(PAIRS1 + 2):
                if i < PAIRS1:
                    s = i % 2
                    pool.wait_ge(exped, i + 1)
                    pool.wait_ge(den_step, 2 * i + 2)
                    for b in range(2):
                        cols, n = (slice(0, P), P) if b == 0 else (slice(P, 3 * P), 2 * P)
                        ins = pool.tensor_tensor(pr1[:, s, :, cols], pr1[:, s, :, cols],
                                                 rden[:, s, 2 * b:2 * b + 2].unsqueeze(2).to_broadcast([P, 2, n]),
                                                 ALU.mult)
                    ins.then_inc(normed, 1)
                if i >= 2:
                    attention_lo(i - 2)
            add_squares(NORM["ffn1"])
            gates("up1", NORM["ffn1"], 1)
            add_squares(NORM["pre2"])

            def rope(j):
                src, t = (q2, j) if j < 8 else (k2, j - 8)
                rows = src[0:ROWS, t, :]
                pool.wait_ge(scaled, SCALED["q2" if j < 8 else "k2"] + t + 1)
                if j >= 2:
                    pool.wait_ge(roped, j - 1)
                pool.tensor_tensor(rtmp[:, j % 2, 0, :], rows, con("cos", TOK, ROWS), ALU.mult).then_inc(rot_cos, 1)
                pool.wait_ge(rot_out, j + 1)
                pool.tensor_tensor(rtmp[:, j % 2, 1, :], rtmp[:, j % 2, 1, :], con("sin", TOK, ROWS), ALU.mult)\
                    .then_inc(rot_prod, 1)
                pool.wait_ge(rot_cos, j + 1)
                pool.wait_ge(rot_prod, j + 1)
                pool.tensor_tensor(rows, rtmp[:, j % 2, 0, :], rtmp[:, j % 2, 1, :], ALU.add).then_inc(roped, 1)

            def scale(name, t):
                dst = vfm[:, t % 2, :] if name == "v2" else DST[name][:, t, :]
                pool.wait_ge(summed, T0[name] + t + 1)
                pool.tensor_tensor(dst, dst, rbc[:], ALU.mult).then_inc(pool_scaled, 1)

            for j in range(16):
                rope(j)
            pool.wait_ge(xc_lo, KT)

            def gated_input(t):
                pool.wait_ge(i_ready, t // 4 + 1)
                pool.tensor_tensor(xc[:, t, :], xc[:, t, :], ga[:, t, :], ALU.mult).then_inc(ix_ready, 1)

            for t in range(4):
                gated_input(t)
            for t in range(KT):
                scale("v2", t)
                if t < 4:
                    gated_input(4 + t)
            for t in range(KT):
                scale("g2", t)
            for t in range(KT):
                scale("ga", t)
                if 2 <= t < 6:
                    for k in (2 * t - 4, 2 * t - 3):
                        pool.wait_ge(mult_ready, 1 if k < 6 else 2)
                        pool.wait_ge(ix_ready, k + 1)
                        pool.tensor_tensor(xl[:, k, 0:TOK], xl[:, k, 0:TOK], xc[:, k, :], ALU.mult)\
                            .then_inc(bx_ready, 1)
            for t in range(KT):
                scale("gl", t)
                if t == 5:
                    pool.wait_ge(gelu_ready, 1)
                for k in {5: (0, 1, 2), 6: (3, 4, 5), 7: (6, 7)}.get(t, ()):
                    pool.wait_ge(scanned, k + 1)
                    pool.tensor_tensor(xc[:, k, :], xc[:, k, :], g2[:, k, :], ALU.mult).then_inc(lru_ready, 1)
            for t in range(KT):
                pool.wait_ge(gated_att, t + 1)
                pool.wait_ge(gated_lru, t + 1)
                pool.tensor_tensor(z[:, t % 4, :], z[:, t % 4, :], ga[:, t, :], ALU.add).then_inc(merged, 1)
            add_squares(NORM["post2"])
            add_squares(NORM["mpre"])
            pool.wait_ge(rbc2_ready, 1)

            def square_relu(i):
                for p in range(4):
                    pool.wait_ge(relu_ready, 4 * i + p + 1)
                    pool.tensor_tensor(z[:, p, :], z[:, p, :], rbc2[:], ALU.mult).then_inc(sqrelu_ready, 1)
            repeat(pool, 8, square_relu)
            add_squares(NORM["mpost"])
            pool.wait_ge(rbc_ready, NORM["mpost"] + 1)
            pool.wait_ge(gained, 2)
            for t in (6, 7):
                pool.tensor_tensor(mres[:, t, :], mres[:, t, :], rbc[:], ALU.mult).then_inc(end_step, 1)
                pool.wait_ge(end_step, t - 5)
                pool.tensor_tensor(x[:, t, :], x[:, t, :], mres[:, t, :], ALU.add).then_inc(final_pool, 1)


def _tiles(v):
    return np.asarray(v).reshape(-1, P).T


def _chunk(w, rows, cols):
    part = w[rows][:, cols]
    return part.reshape(-1, P, 2, P).transpose(1, 2, 0, 3).reshape(-1)


def _stream(w):
    out = []

    def columns(m, cols, rows=slice(0, D)):
        out.append(_chunk(m, rows, cols))

    def cols(start):
        return np.arange(start, start + 2 * P)

    def gated(layer):
        gu, dn = w["ffn_w_gate_up"][layer], w["ffn_w_down"][layer]
        for j in range(FF // 256):
            columns(gu, cols(256 * j))
            columns(gu, cols(FF + 256 * j))
        for g in range(4):
            for k0, kts in GROUP_K:
                columns(dn, cols(256 * g), slice(k0 * P, (k0 + kts) * P))

    w_in = w["conv_w_in"][0]
    for j in range(4):
        columns(w_in, cols(256 * j))
        columns(w_in, cols(2 * D + 256 * j))
    for j in range(4):
        columns(w_in, cols(D + 256 * j))
    for j in range(4):
        columns(w["conv_w_out"][0], cols(256 * j))
    gated(0)
    order = np.concatenate([np.arange(HD1 * head1(i), HD1 * head1(i) + HD1) for i in range(HEADS1)])
    qkv = w["attn_w_qkv"][0]
    order_all = np.concatenate([np.arange(D, D + 2 * KV1 * HD1), order])
    for j in range(6):
        columns(qkv, order_all[256 * j:256 * j + 256])
    wo = w["attn_w_o"][0][order]
    for j in range(4):
        columns(wo, cols(256 * j))
    gated(1)
    w_in = w["w_in_2"][0]
    part = {"q2": 0, "k2": 1, "v2": 2, "x2": 3, "g2": 4, "ga": 5, "gl": 6}
    for name in ("x2", "q2", "k2", "rg", "v2", "g2", "ga", "gl"):
        if name == "rg":
            for m in (w["w_rg_a_2"][0], w["w_rg_i_2"][0]):
                six = m.reshape(2, 2, 2, P, 2, P)
                out.append(six.transpose(3, 0, 1, 4, 2, 5).reshape(-1))
        else:
            rows = np.arange(D).reshape(HEADS2, HD2)
            if name in ("q2", "k2"):
                rows = rows[:, list(range(16)) + list(range(32, 48)) + list(range(16, 32)) + list(range(48, HD2))]
            rows = rows.reshape(-1)
            for j in range(4):
                columns(w_in, D * part[name] + rows[256 * j:256 * j + 256])
    for name in ("w_branch_attn_2", "w_branch_lru_2", "w_out_2"):
        for j in range(4):
            columns(w[name][0], cols(256 * j))
    for j in range(FF2 // 256):
        columns(w["w_mlp_up_2"][0], cols(256 * j))
    for g in range(4):
        for c in range(4):
            columns(w["w_mlp_down_2"][0], cols(256 * g), slice(c * D, (c + 1) * D))
    return np.concatenate(out)


def _constants():
    c = np.zeros((P, NCON), np.float32)
    c[:, 0:P] = 1.0
    c[0:64, 128:192] = 1.0
    c[64:128, 192:256] = 1.0
    c[:, 256:384] = np.eye(P, dtype=np.float32)
    q, k = np.arange(P)[:, None], np.arange(P)[None, :]
    c[:, 384:768] = np.concatenate([np.where(q >= k, 0, -BIG), np.zeros((P, P)), np.where(q >= k, 0, -BIG)], 1)
    half = ROT // 2
    freq = np.float32(500000.0) ** (-np.arange(0, ROT, 2, dtype=np.float32) / np.float32(ROT))
    angle = np.arange(TOK, dtype=np.float32)[:, None] * freq.astype(np.float32)[None, :]
    c[0:ROWS, 768:1024] = 1.0
    for first, sign in ((0, -1.0), (32, 1.0)):
        c[first:first + half, 768:1024] = np.cos(angle).T
        c[first:first + half, 1024:1280] = sign * np.sin(angle).T
    return c


def _bias():
    q, k = np.arange(P)[:, None], np.arange(P)[None, :]
    own = np.where(q >= k, q - k, BIG)
    before = np.where(k > q, q + P - k, BIG)
    dist = np.concatenate([own, before, own], 1).astype(np.float32)
    slopes = [np.float32(2.0) ** np.float32(-8.0 * (head1(i) + 1) / HEADS1) for i in range(HEADS1)]
    return np.concatenate([-s * dist for s in slopes], 1)


_NAMES = ["bias", "x", "stream", "vecs", "sinks", "cons"]


def kernel(**inputs):
    import concourse.bacc as _bacc
    from concourse.bass_utils import run_bass_kernel_spmd as _run

    w = {k: np.asarray(v) for k, v in inputs.items()}
    f = _tiles
    vecs = [f(w["norm_mixer"][0]), f(w["norm_ffn"][0]), f(w["norm_mixer"][1]), f(w["norm_ffn"][1]),
            f(w["conv_w"][0][0]), f(w["conv_w"][0][1]), f(w["conv_w"][0][2]),
            f(np.concatenate([w["attn_q_gain"][0]] * 2)), f(np.concatenate([w["attn_k_gain"][0]] * 2)),
            f(w["attn_pre_norm_2"][0]), f(w["attn_post_norm_2"][0]),
            *[f(w["conv_w_2"][0][j]) for j in range(4)], f(w["conv_b_2"][0]),
            f(w["b_rg_a_2"][0]), f(w["b_rg_i_2"][0]), f(w["lru_lambda_2"][0]),
            f(w["mlp_pre_norm_2"][0]), f(w["mlp_post_norm_2"][0])]
    arrays = {
        "x": w["x"][0].T.reshape(KT, P, TOK).transpose(1, 0, 2),
        "stream": _stream(w),
        "vecs": np.concatenate(vecs, 1),
        "sinks": np.broadcast_to(w["attn_sinks"][0][[head1(2 * t + h) for t in range(PAIRS1) for _ in range(2)
                                                     for h in range(2)]][None, :], (P, 4 * PAIRS1)),
        "bias": _bias(),
        "cons": _constants(),
    }
    nc = _bacc.Bacc("TRN2", target_bir_lowering=False, num_devices=1, dynamic_dma_scratch_size=1024)
    held, args = {}, []
    for name in _NAMES:
        a = np.ascontiguousarray(arrays[name])
        held[f"in_{name}"] = a
        args.append(nc.dram_tensor(f"in_{name}", a.shape, mybir.dt.from_np(a.dtype), kind="ExternalInput").ap())
    args.append(nc.dram_tensor("out_0", (P, KT, TOK), F32, kind="ExternalOutput").ap())
    build(nc, *args)
    r = _run(nc, [held], core_ids=[0])
    got = r.results[0]["out_0"]
    return np.ascontiguousarray(got.transpose(1, 0, 2).reshape(D, TOK).T)[None]
```
